# Optimizing a Trainium2 kernel written in Bass

```python
import math
import jax, jax.numpy as jnp
from jax import lax
import numpy as np

D_MODEL = 2048
BATCH = 1
SEQ = 256
DEPTH = 2

N_MIXERS = 2
N_DN_LAYERS = (DEPTH + 1) // 2
N_S5_LAYERS = DEPTH // 2

DN_K_HEADS = 16
DN_V_HEADS = 32
DN_HEAD_DIM = 128
DN_KEY_DIM = DN_K_HEADS * DN_HEAD_DIM
DN_VAL_DIM = DN_V_HEADS * DN_HEAD_DIM
DN_CONV_DIM = 2 * DN_KEY_DIM + DN_VAL_DIM
DN_CONV_K = 5
DN_CHUNK = 64
DN_IN_DIM = DN_CONV_DIM + DN_VAL_DIM + 4 * DN_V_HEADS

S5_GROUP = 16
S5_GROUPS = D_MODEL // S5_GROUP
S5_STATE = 64
S5_DT_MIN = 1e-3
S5_DT_MAX = 1e-1

FFN_HIDDEN = -(-8 * D_MODEL // (3 * 256)) * 256
RMS_EPS = 1e-6

kernel_name = "hybrid_deltanet_s5_encoder"

def rms_norm(x, w):
    xf = x.astype(jnp.float32)
    y = xf * lax.rsqrt(jnp.mean(xf * xf, axis=-1, keepdims=True) + RMS_EPS)
    return (y * w.astype(jnp.float32)).astype(x.dtype)

def l2norm(x):
    xf = x.astype(jnp.float32)
    return xf * lax.rsqrt(jnp.sum(xf * xf, axis=-1, keepdims=True) + 1e-6)

def centred_depthwise_conv(x, w):
    k, ch = w.shape
    return lax.conv_general_dilated(
        x, w[:, None, :].astype(x.dtype), window_strides=(1,),
        padding=[(k // 2, k // 2)], dimension_numbers=("NWC", "WIO", "NWC"),
        feature_group_count=ch)

def chunk_gated_delta_rule(q, k, v, g, beta):
    f32 = jnp.float32
    bsz, seq, nh, dk = q.shape
    dv = v.shape[-1]
    n = seq // DN_CHUNK

    def chunks(t):
        return t.reshape((bsz, n, DN_CHUNK) + t.shape[2:]).swapaxes(2, 3)

    q = chunks(q.astype(f32) * (dk ** -0.5))
    k = chunks(k.astype(f32))
    v = chunks(v.astype(f32))
    g = jnp.cumsum(chunks(g.astype(f32)), axis=-1)
    beta = chunks(beta.astype(f32))[..., None]
    k_beta = k * beta
    v_beta = v * beta

    lower = jnp.tril(jnp.ones((DN_CHUNK, DN_CHUNK), dtype=bool))
    strict = jnp.tril(jnp.ones((DN_CHUNK, DN_CHUNK), dtype=bool), -1)
    decay = jnp.exp(jnp.where(lower, g[..., :, None] - g[..., None, :], -jnp.inf))

    a_kk = jnp.einsum("bnhid,bnhjd->bnhij", k_beta, k) * decay
    eye = jnp.eye(DN_CHUNK, dtype=f32)
    m = jnp.where(strict, a_kk, 0.0) + eye
    rhs = jnp.concatenate([v_beta, k_beta * jnp.exp(g)[..., None]], axis=-1)
    sol = lax.linalg.triangular_solve(m, rhs, left_side=True, lower=True, unit_diagonal=True)
    u, w = sol[..., :dv], sol[..., dv:]

    a_qk = jnp.einsum("bnhid,bnhjd->bnhij", q, k) * decay
    q_g = q * jnp.exp(g)[..., None]
    g_last = g[..., -1]
    k_tail = k * jnp.exp(g_last[..., None] - g)[..., None]

    def step(state, inp):
        qg, wc, uc, aqk, kt, gl = inp
        v_new = uc - jnp.einsum("bhcd,bhde->bhce", wc, state)
        o = jnp.einsum("bhcd,bhde->bhce", qg, state) + jnp.einsum("bhij,bhje->bhie", aqk, v_new)
        state = state * jnp.exp(gl)[..., None, None] + jnp.einsum("bhcd,bhce->bhde", kt, v_new)
        return state, o

    xs = tuple(t.swapaxes(0, 1) for t in (q_g, w, u, a_qk, k_tail, g_last))
    state0 = jnp.zeros((bsz, nh, dk, dv), f32)
    _, o = lax.scan(step, state0, xs)
    return o.transpose(1, 0, 3, 2, 4).reshape(bsz, seq, nh, dv)

def gated_deltanet_mixer(h, w_in, conv_w, a_log, dt_bias, norm_w, w_out):
    f32 = jnp.float32
    bsz, seq, _ = h.shape
    proj = h @ w_in
    qkv, z, ab = jnp.split(proj, [DN_CONV_DIM, DN_CONV_DIM + DN_VAL_DIM], axis=-1)
    qkv = jax.nn.silu(centred_depthwise_conv(qkv, conv_w))
    q, k, v = jnp.split(qkv, [DN_KEY_DIM, 2 * DN_KEY_DIM], axis=-1)
    rep = DN_V_HEADS // DN_K_HEADS
    q = jnp.repeat(l2norm(q.reshape(bsz, seq, DN_K_HEADS, DN_HEAD_DIM)), rep, axis=2)
    k = jnp.repeat(l2norm(k.reshape(bsz, seq, DN_K_HEADS, DN_HEAD_DIM)), rep, axis=2)
    v = v.reshape(bsz, seq, DN_V_HEADS, DN_HEAD_DIM)

    ab = ab.astype(f32).reshape(bsz, seq, 2, 2, DN_V_HEADS)
    beta = jax.nn.sigmoid(ab[:, :, :, 0])
    g = -jnp.exp(a_log.astype(f32)) * jax.nn.softplus(ab[:, :, :, 1] + dt_bias.astype(f32))

    o_fwd = chunk_gated_delta_rule(q, k, v, g[:, :, 0], beta[:, :, 0])
    flip = lambda t: jnp.flip(t, axis=1)
    o_bwd = flip(chunk_gated_delta_rule(flip(q), flip(k), flip(v), flip(g[:, :, 1]), flip(beta[:, :, 1])))
    o = o_fwd + o_bwd

    z = z.reshape(bsz, seq, DN_V_HEADS, DN_HEAD_DIM).astype(f32)
    o = rms_norm(o, norm_w) * jax.nn.silu(z)
    return o.reshape(bsz, seq, DN_VAL_DIM).astype(h.dtype) @ w_out

def s5_direction(u, lam_re, lam_im, log_step, b_re, b_im, c_re, c_im, reverse):
    f32 = jnp.float32
    seq = u.shape[1]
    lam = lax.complex(lam_re.astype(f32), lam_im.astype(f32))
    step = jnp.exp(log_step.astype(f32))[:, None]
    lam_bar = jnp.exp(lam * step)
    b = lax.complex(b_re.astype(f32), b_im.astype(f32))
    b_bar = ((lam_bar - 1.0) / lam)[..., None] * b
    bu = lax.complex(jnp.einsum("gpc,blgc->blgp", jnp.real(b_bar), u),
                     jnp.einsum("gpc,blgc->blgp", jnp.imag(b_bar), u))
    a = jnp.broadcast_to(lam_bar, (seq,) + lam_bar.shape)

    def combine(e1, e2):
        a1, b1 = e1
        a2, b2 = e2
        return a2 * a1, a2 * b1 + b2

    def scan_one(bu_seq):
        return lax.associative_scan(combine, (a, bu_seq), reverse=reverse, axis=0)[1]

    xs = jax.vmap(scan_one)(bu)
    return (jnp.einsum("gcp,blgp->blgc", c_re.astype(f32), jnp.real(xs))
            - jnp.einsum("gcp,blgp->blgc", c_im.astype(f32), jnp.imag(xs)))

def s5_mixer(h, w_in, lam_re, lam_im, log_step, b_re, b_im, c_re, c_im, d_skip, w_glu, w_out):
    f32 = jnp.float32
    bsz, seq, _ = h.shape
    u = (h @ w_in).astype(f32)
    ug = u.reshape(bsz, seq, S5_GROUPS, S5_GROUP)
    y_f = s5_direction(ug, lam_re[0], lam_im[0], log_step[0], b_re[0], b_im[0], c_re[0], c_im[0], False)
    y_b = s5_direction(ug, lam_re[1], lam_im[1], log_step[1], b_re[1], b_im[1], c_re[1], c_im[1], True)
    y = (y_f + y_b).reshape(bsz, seq, D_MODEL) + d_skip.astype(f32) * u
    y = jax.nn.gelu(y, approximate=False).astype(h.dtype)
    y = y * jax.nn.sigmoid(y @ w_glu)
    return y @ w_out

def swiglu(h, w_gate, w_up, w_down):
    return (jax.nn.silu(h @ w_gate) * (h @ w_up)) @ w_down

def setup_inputs(seed: int = 0) -> dict:
    key = jax.random.key(seed)
    ks = iter(jax.random.split(key, 40))
    nrm = lambda shape, s: jax.random.normal(next(ks), shape, jnp.float32) * s
    gain = lambda shape: 1.0 + nrm(shape, 0.05)
    D, F = D_MODEL, FFN_HIDDEN
    G, P, Q = S5_GROUPS, S5_STATE, S5_GROUP
    nd, ns = N_DN_LAYERS, N_S5_LAYERS
    return {
        "x": nrm((BATCH, SEQ, D), 1.0),
        "c": nrm((BATCH, D), 1.0),
        "mod_w": nrm((DEPTH, D, 6 * D), D ** -0.5),
        "mod_b": nrm((DEPTH, 6 * D), 0.01),
        "norm_pre_mix": gain((DEPTH, D)),
        "norm_post_mix": gain((DEPTH, D)),
        "norm_pre_ffn": gain((DEPTH, D)),
        "norm_post_ffn": gain((DEPTH, D)),
        "dn_w_in": nrm((nd, D, DN_IN_DIM), D ** -0.5),
        "dn_conv_w": nrm((nd, DN_CONV_K, DN_CONV_DIM), DN_CONV_K ** -0.5),
        "dn_a_log": jnp.log(jax.random.uniform(next(ks), (nd, 2, DN_V_HEADS), jnp.float32, 1.0, 16.0)),
        "dn_dt_bias": 1.0 + nrm((nd, 2, DN_V_HEADS), 0.1),
        "dn_norm_w": gain((nd, DN_HEAD_DIM)),
        "dn_w_out": nrm((nd, DN_VAL_DIM, D), DN_VAL_DIM ** -0.5),
        "s5_w_in": nrm((ns, D, D), D ** -0.5),
        "s5_lam_re": -0.5 * jnp.exp(nrm((ns, 2, G, P), 0.05)),
        "s5_lam_im": math.pi * jnp.arange(P, dtype=jnp.float32) + nrm((ns, 2, G, P), 0.05),
        "s5_log_step": jax.random.uniform(next(ks), (ns, 2, G), jnp.float32,
                                          math.log(S5_DT_MIN), math.log(S5_DT_MAX)),
        "s5_b_re": nrm((ns, 2, G, P, Q), (2 * Q) ** -0.5),
        "s5_b_im": nrm((ns, 2, G, P, Q), (2 * Q) ** -0.5),
        "s5_c_re": nrm((ns, 2, G, Q, P), (2 * P) ** -0.5),
        "s5_c_im": nrm((ns, 2, G, Q, P), (2 * P) ** -0.5),
        "s5_d": nrm((ns, D), 1.0),
        "s5_w_glu": nrm((ns, D, D), D ** -0.5),
        "s5_w_out": nrm((ns, D, D), D ** -0.5),
        "ffn_w_gate": nrm((DEPTH, D, F), D ** -0.5),
        "ffn_w_up": nrm((DEPTH, D, F), D ** -0.5),
        "ffn_w_down": nrm((DEPTH, F, D), F ** -0.5),
    }

def reference(x, c, mod_w, mod_b, norm_pre_mix, norm_post_mix, norm_pre_ffn, norm_post_ffn,
              dn_w_in, dn_conv_w, dn_a_log, dn_dt_bias, dn_norm_w, dn_w_out,
              s5_w_in, s5_lam_re, s5_lam_im, s5_log_step, s5_b_re, s5_b_im, s5_c_re, s5_c_im,
              s5_d, s5_w_glu, s5_w_out, ffn_w_gate, ffn_w_up, ffn_w_down):
    cond = jax.nn.silu(c)
    for i in range(DEPTH):
        mod = (cond @ mod_w[i] + mod_b[i])[:, None, :]
        sh_m, sc_m, gt_m, sh_f, sc_f, gt_f = jnp.split(mod, 6, axis=-1)

        h = rms_norm(x, norm_pre_mix[i]) * (1.0 + sc_m) + sh_m
        j = i // N_MIXERS
        if i % N_MIXERS == 0:
            out = gated_deltanet_mixer(h, dn_w_in[j], dn_conv_w[j], dn_a_log[j], dn_dt_bias[j],
                                       dn_norm_w[j], dn_w_out[j])
        else:
            out = s5_mixer(h, s5_w_in[j], s5_lam_re[j], s5_lam_im[j], s5_log_step[j],
                           s5_b_re[j], s5_b_im[j], s5_c_re[j], s5_c_im[j], s5_d[j],
                           s5_w_glu[j], s5_w_out[j])
        x = x + gt_m * rms_norm(out, norm_post_mix[i])

        h = rms_norm(x, norm_pre_ffn[i]) * (1.0 + sc_f) + sh_f
        out = swiglu(h, ffn_w_gate[i], ffn_w_up[i], ffn_w_down[i])
        x = x + gt_f * rms_norm(out, norm_post_ffn[i])
    return x


_drawn_inputs = setup_inputs


def setup_inputs(seed=0):
    import zlib

    import numpy as np

    out = dict(_drawn_inputs(seed))
    spreads = {}
    factors = {'dn_dt_bias': 62.168,
     's5_lam_re': 200.0,
     'dn_a_log': 8.0,
     's5_lam_im': 28.664,
     's5_log_step': 38.072,
     's5_b_re': 38.264,
     's5_b_im': 38.4,
     's5_c_re': 38.632,
     's5_c_im': 38.16}
    for name, (base, spread) in spreads.items():
        noise = np.random.default_rng([zlib.crc32(name.encode()), seed]).standard_normal(out[name].shape)
        drawn = base * np.exp(spread * noise) if base else spread * noise
        out[name] = __import__('jax').numpy.asarray(drawn.astype(out[name].dtype))
    for name, factor in factors.items():
        out[name] = (out[name] * factor).astype(out[name].dtype)
    return out
```

```python
import math
from contextlib import ExitStack

import concourse.bass as bass
from concourse import mybir

ALU = mybir.AluOpType
ACT = mybir.ActivationFunctionType
F32 = mybir.dt.float32
F32R = mybir.dt.float32r
I32 = mybir.dt.int32
AX_X = mybir.AxisListType.X
ds = bass.ds

P = 128
ARENA = 27152
RAW = 2
TILE = 2048
ROUND = 12582912.0
RSQRT_SEED = float(0x5F3759DF)
EPS = 1e-6
TWO_PI = 6.2831845
HEAD_LINKS = 44
S5_LINKS = 18
S5OUT = (14, 8, 19, 21)


class Chain:

    def __init__(self, eng, sem):
        self.eng, self.sem, self.n, self.off = eng, sem, 0, 0

    def link(self, ins):
        ins.then_inc(self.sem, 1)
        self.n += 1
        self.eng.wait_ge(self.sem, self.off + self.n)

    def enter(self, i, per):
        self.off, self.start = i * per, self.n

    def leave(self, per, trips):
        assert self.n - self.start == per, (self.n - self.start, per)
        self.n, self.off = self.start + per * trips, 0


def trunk(nc, a, out):
    T, D = a["x"].shape[1], a["x"].shape[2]
    KT = D // P
    NT = T // P
    FT = a["ffn_w_gate"].shape[2] // P
    VH = a["dn_a_log"].shape[2]
    KH = VH // 2
    DV = VH * P
    QOFF, KOFF, VOFF, ZOFF, ABOFF = 0, KH * P, 2 * KH * P, 2 * KH * P + DV, 2 * KH * P + 2 * DV
    CK = a["dn_conv_w"].shape[1]
    PAD = CK // 2
    G, PS, Q = a["s5_b_re"].shape[2:5]
    GP = G // 2
    NJ = G * Q // P
    LV = 6
    DK_SCALE = float(P) ** -0.5
    assert T == 2 * P and D == 2048 and NT == 2 and G * PS == GP * P and Q * 8 == P

    ctx = ExitStack()
    with ctx:
        def sb(name, cols, dt=F32):
            return ctx.enter_context(nc.sbuf_tensor(name, [P, cols], dt))[:, :]

        def sem(name):
            return ctx.enter_context(nc.semaphore(name))

        def dram(name, shape):
            return nc.dram_tensor(name, shape, F32).ap()

        raw = sb("raw", RAW * TILE).rearrange("p (s n) -> p s n", s=RAW)
        whi = sb("whi", 2 * TILE, F32R).rearrange("p (s n) -> p s n", s=2)
        wlo = sb("wlo", 2 * TILE, F32R).rearrange("p (s n) -> p s n", s=2)
        hhi = sb("hhi", KT * T, F32R).rearrange("p (k t) -> p k t", k=KT)
        hlo = sb("hlo", KT * T, F32R).rearrange("p (k t) -> p k t", k=KT)
        shi = sb("shi", 2 * T, F32R).rearrange("p (s t) -> p s t", s=2)
        slo = sb("slo", 2 * T, F32R).rearrange("p (s t) -> p s t", s=2)
        ident = sb("ident", P)
        ones = sb("ones", P)
        normc = sb("normc", 128)
        modb = sb("modb", 192).rearrange("p (l n) -> p l n", l=2)
        modc = sb("modc", 192).rearrange("p (l n) -> p l n", l=2)
        misc = sb("misc", 33)
        cond = sb("cond", KT)
        acol = sb("acol", KT)
        gwcol = sb("gwcol", KT)
        small = sb("small", 64)
        tbl = sb("tbl", 4 * 128).rearrange("p (k h u) -> p k h u", k=4, h=KH)
        cols = sb("cols", 32).rearrange("p (k u) -> p k u", k=4)
        convw = sb("convw", 320).rearrange("p (j t) -> p j t", j=CK)
        convh = sb("convh", 20).rearrange("p (t j) -> p t j", t=4)
        mkq = sb("mkq", 512).rearrange("p (d m i) -> p d m i", d=2, m=2)
        m1 = sb("m1", 256).rearrange("p (d i) -> p d i", d=2)
        mlv = sb("mlv", 2 * LV * 64).rearrange("p (l d n) -> p l d n", l=LV, d=2)
        junk = sb("junk", 512)

        ps = ctx.enter_context(nc.psum_tensor("ps", [P, 8, 512], F32))[:, :, :]

        A = ctx.enter_context(nc.sbuf_tensor("arena", [P, ARENA], F32))[:, :]
        taken = [0]

        def region(at, n):
            assert at + n <= ARENA, at + n
            taken[0] = at + n
            return A[:, at:at + n]

        def four(v, n):
            return v.rearrange("p (u i) -> p u i", u=n)

        oT = region(0, 8192).rearrange("p (k t) -> p k t", k=VH)
        macc = region(8192, 4096).rearrange("p (c n) -> p c n", c=2)
        gwrow_mix = region(22528, 2048)
        yact = region(14336, 1024)
        eD = region(15360, 1024)
        qkn = four(region(16384, 512), 4)
        qkT = four(region(16896, 512), 4)
        km = region(17408, 1024).rearrange("p (d m c i) -> p d m c i", d=2, m=2, c=2)
        grow = four(region(18432, 1024), 8)
        brow = four(region(19456, 1024), 8)
        Bm = four(region(20480, 1024), 8)
        Aqk = four(region(21504, 1024), 8)
        Sm = four(region(22528, 1024), 8)
        Tm = four(region(23552, 1024), 8)
        Xm = region(24576, 512).rearrange("p (d u n) -> p d u n", d=2, u=4)
        Vb = four(region(25088, 1024), 8)
        R1 = region(12288, 512).rearrange("p (d v i) -> p d v i", d=2, v=2)
        Kt = region(12800, 512).rearrange("p (d v i) -> p d v i", d=2, v=2)
        Ssb = region(13312, 512).rearrange("p (d v i) -> p d v i", d=2, v=2)
        Vn = four(region(26112, 1024), 8)
        cbuf = region(26112, 1040).rearrange("p (t n) -> p t n", t=4)
        QSs = four(A[:, 18432:18944], 4)
        Osb = four(A[:, 18944:19456], 4)
        zth = four(A[:, 26112:26624], 4)
        zg = four(A[:, 13824:14336], 4)
        abw = region(15360, 2048).rearrange("p (n t) -> p n t", n=8)
        diag = region(19456, 2048).rearrange("p (g u i) -> p g u i", g=4, u=4)
        ptmp = region(17408, 4096).rearrange("p (c n) -> p c n", c=2)
        htmp = region(21504, 512).rearrange("p (s t) -> p s t", s=2)
        hid = region(0, 11264).rearrange("p (k t) -> p k t", k=FT)
        gwrow_ffn = region(11264, 2048)
        macc4 = region(13312, 8192).rearrange("p (c n) -> p c n", c=4)
        fth = region(21504, 1024).rearrange("p (s n) -> p s n", s=2)
        ftt = region(22528, 1024).rearrange("p (s n) -> p s n", s=2)
        xbuf = region(0, 4096).rearrange("p (c n) -> p c n", c=2)
        xn = region(4096, 4096).rearrange("p (c n) -> p c n", c=2)
        pin = region(14336, 1024).rearrange("p (n i) -> p n i", n=8)
        uT = region(0, 4096).rearrange("p (k t) -> p k t", k=KT)
        ysb = region(4096, 4096).rearrange("p (k t) -> p k t", k=KT)
        bnat = region(8192, 4096).rearrange("p (r n) -> p r n", r=2)
        cnat = region(12288, 4096).rearrange("p (r d j s) -> p r d j s", r=2, d=2, j=NJ)
        s5p = region(16384, 1024).rearrange("p (n i) -> p n i", n=8)
        gmask = region(17408, 256).rearrange("p (s i) -> p s i", s=2)
        iota = region(17664, 256)
        uj = region(17920, 256)
        cj = region(18176, 1024).rearrange("p (s n) -> p s n", s=2)
        bx = region(19200, 512).rearrange("p (n i) -> p n i", n=4)
        bT = region(19712, 512).rearrange("p (n i) -> p n i", n=4)
        cdup = region(20224, 512).rearrange("p (n i) -> p n i", n=4)
        trig = region(20736, 1536).rearrange("p (s n t) -> p s n t", s=2, n=3)
        ang = region(22272, 512).rearrange("p (s t) -> p s t", s=2)
        kb = region(22784, 256)
        kc = region(23040, 256)
        angabs = region(26640, 512).rearrange("p (s t) -> p s t", s=2)
        tc_ = region(23552, 512).rearrange("p (n t) -> p n t", n=2)
        ts_ = region(24064, 512).rearrange("p (n t) -> p n t", n=2)
        zin = region(24576, 512).rearrange("p (n t) -> p n t", n=2)
        zst = region(25088, 512).rearrange("p (n t) -> p n t", n=2)
        pcos = region(25600, 512).rearrange("p (n t) -> p n t", n=2)
        psin = region(26112, 512).rearrange("p (n t) -> p n t", n=2)
        colj = cols.rearrange("p k u -> p (k u)")
        s5w = region(17920, 4096).rearrange("p (n i) -> p n i", n=32)

        x_dram = [dram(f"x_resid{s}", [T, D]) for s in range(3)]
        g_rows = dram("g_rows", [2 * VH, T])
        b_rows = dram("b_rows", [2 * VH, T])

        raw_landed = [sem(f"raw_landed{s}") for s in range(RAW)]
        raw_used = sem("raw_used")
        hi_ready = sem("hi_ready")
        w_used = sem("w_used")
        acts = sem("act_chain")
        dves = sem("dve_chain")
        pools = sem("pool_chain")
        consts_ready = sem("consts_ready")
        params_in = sem("params_in")
        params_T = sem("params_T")
        params_ready = sem("params_ready")
        macc_zero = sem("macc_zero")
        mod_ps = sem("mod_ps")
        mod_ready = sem("mod_ready")
        diag_ready = sem("diag_ready")
        gw_ps = sem("gw_ps")
        gw_ready = sem("gw_ready")
        x_landed = sem("x_landed")
        x_stored = sem("x_stored")
        ss_out = sem("ss_out")
        x_new = sem("x_new")
        ss_x = sem("ss_x")
        rstd_x = sem("rstd_x")
        xn_ready = sem("xn_ready")
        xnT_ps = sem("xnT_ps")
        h_hi = sem("h_hi")
        h_ready = sem("h_ready")
        ab_act = sem("ab_act")
        ab_dve = sem("ab_dve")
        gT_ps = sem("gT_ps")
        rows_stored = sem("rows_stored")
        tbl_ready = sem("tbl_ready")
        cbuf_ready = sem("cbuf_ready")
        conv_done = sem("conv_done")
        zg_ready = sem("zg_ready")
        ymm = sem("ymm")
        silu_tanh = sem("silu_tanh")
        act_done = sem("act_done")
        tok_ps = sem("tok_ps")
        ss_ready = sem("ss_ready")
        qkn_ready = sem("qkn_ready")
        vb_ready = sem("vb_ready")
        qkT_ps = sem("qkT_ps")
        qkT_ready = sem("qkT_ready")
        kk_ps = sem("kk_ps")
        km_ready = sem("km_ready")
        rows_landed = sem("rows_landed")
        de_ready = sem("de_ready")
        e_ready = sem("e_ready")
        eb_ready = sem("eb_ready")
        aqk_ready = sem("aqk_ready")
        s0_ready = sem("s0_ready")
        t0_ps = sem("t0_ps")
        t0_ready = sem("t0_ready")
        x_ps = sem("x_ps")
        xm_ready = sem("xm_ready")
        y_ps = sem("y_ps")
        t_ready = sem("t_ready")
        tt_ps = sem("tt_ps")
        s_ready = sem("s_ready")
        ktail_ready = sem("ktail_ready")
        u0_ps = sem("u0_ps")
        u0_ready = sem("u0_ready")
        st_ps = sem("st_ps")
        st_ready = sem("st_ready")
        ks_ps = sem("ks_ps")
        r1_ready = sem("r1_ready")
        qs_ready = sem("qs_ready")
        v1_ps = sem("v1_ps")
        v1_ready = sem("v1_ready")
        o_ps = sem("o_ps")
        o_ready = sem("o_ready")
        oss_ready = sem("oss_ready")
        z_tanh = sem("z_tanh")
        og_ready = sem("og_ready")
        oT_ps = sem("oT_ps")
        oT_ready = sem("oT_ready")
        gate_tanh = sem("gate_tanh")
        gate_used = sem("gate_used")
        hid_ready = sem("hid_ready")
        fm_done = sem("fm_done")
        s5_in = sem("s5_in")
        s5_act = sem("s5_act")
        s5_dve = sem("s5_dve")
        s5_dve_a = sem("s5_dve_a")
        s5_act_a = sem("s5_act_a")
        abs_done = sem("abs_done")
        s5_psT = sem("s5_psT")
        s5_ready = sem("s5_ready")
        bx_ready = sem("bx_ready")
        cdup_ready = sem("cdup_ready")
        bcT_ps = sem("bcT_ps")
        bT_ready = sem("bT_ready")
        cj_ready = sem("cj_ready")
        uj_ready = sem("uj_ready")
        ang_ready = sem("ang_ready")
        trig_ready = sem("trig_ready")
        bu_ps = sem("bu_ps")
        t_prod = sem("t_prod")
        zin_ready = sem("zin_ready")
        z_ready = sem("z_ready")
        psin_ready = sem("psin_ready")
        pcos_ready = sem("pcos_ready")
        ysum_ready = sem("ysum_ready")
        gelu_done = sem("gelu_done")
        glu_h = sem("glu_h")
        glu_tanh = sem("glu_tanh")

        MODK = a["mod_w"]
        LOOPM = 8
        n_ab = 2 * KT
        n_head = n_ab + 1
        PER_HEAD = 8
        n_dout = n_head + PER_HEAD * KH
        n_gu0 = n_dout + VH + 2 * KT
        n_dn0 = n_gu0 + 2 * 2 * FT // 2 + 4 * KT
        n_sin = n_dn0 + FT + 2 * KT
        n_glu = n_sin + KT
        n_sout = n_glu + KT
        n_gu1 = n_sout + KT
        n_dn1 = n_gu1 + 2 * FT
        m_ab, m_head = 0, 1
        m_dout = m_head + 6 * KH
        m_gu0 = m_dout + VH
        m_dn0 = m_gu0 + 2 * FT
        m_sin = m_dn0 + FT
        m_glu = m_sin + KT
        m_sout = m_glu + KT
        m_gu1 = m_sout + KT
        m_dn1 = m_gu1 + 2 * FT

        post_m = [m_gu0, m_sin, m_gu1, m_dn1 + FT]

        def slot_of(n0, j, ring):
            return (n0 + j) % ring

        def load(sp, n0, i, per, j, src, cols=TILE, view=None):
            s = slot_of(n0, j, RAW)
            if n0 + j >= RAW:
                sp.wait_ge(raw_used, i * per + (n0 + j - RAW + 1))
            dst = raw[:, s, :] if view is None else view(raw[:, s, :])
            sp.dma_start(dst, src).then_inc(raw_landed[s], 16)

        def cols_view(kts):
            return lambda v: v.rearrange("p (k n) -> p k n", k=kts)

        def load_cols(sp, n0, i, per, j, w, k0, kts, c0, width):
            load(sp, n0, i, per, j,
                 w[k0 * P:(k0 + kts) * P, ds(c0, width)].rearrange("(k p) n -> p k n", p=P), view=cols_view(kts))

        def load_rows(sp, n0, i, per, j, w, r0):
            load(sp, n0, i, per, j, w[ds(r0, P), :])

        def load_mod(sp, n0, i, per, j, layer, k, chunk):
            load(sp, n0, i, per, j, MODK[layer, ds(k * P, P), chunk * D:(chunk + 1) * D])

        def landed(eng, n0, i, per, j):
            s = slot_of(n0, j, RAW)
            eng.wait_ge(raw_landed[s], i * (per // RAW * 16) + 16 * ((n0 + j) // RAW + 1))

        def split_hi(act, n0, npr, j, m0, mpr, jm, i):
            landed(act, n0, i, npr, j)
            if m0 + jm >= 2 or not isinstance(i, int):
                act.wait_ge(w_used, i * mpr + (m0 + jm - 1))
            act.activation(whi[:, (m0 + jm) % 2, :], raw[:, slot_of(n0, j, RAW), :],
                           ACT.Identity).then_inc(hi_ready, 1)

        def split_lo(dve, n0, npr, j, m0, mpr, jm, i):
            dve.wait_ge(hi_ready, i * mpr + (m0 + jm + 1))
            dve.tensor_tensor(wlo[:, (m0 + jm) % 2, :], raw[:, slot_of(n0, j, RAW), :],
                              whi[:, (m0 + jm) % 2, :].bitcast(F32), ALU.subtract).then_inc(raw_used, 1)

        def mod_acc(dve, n0, i, per, j, acc, k):
            landed(dve, n0, i, per, j)
            if n0 + j > 0:
                dve.wait_ge(raw_used, i * per + (n0 + j))
            s = slot_of(n0, j, RAW)
            dve.scalar_tensor_tensor(out=acc, in0=raw[:, s, :], scalar=cond[:, ds(k, 1)], in1=acc,
                                     op0=ALU.mult, op1=ALU.add).then_inc(raw_used, 1)

        def split_ready(pe, n0, npr, j, m0, mpr, jm, i):
            pe.wait_ge(raw_used, i * npr + (n0 + j + 1))

        def three(pe, o, lh, ll, rh, rl, start, stop):
            pe.matmul(o, lh, rh, start=start, stop=False, skip_group_check=True)
            pe.matmul(o, lh, rl, start=False, stop=False, skip_group_check=True)
            return pe.matmul(o, ll, rh, start=False, stop=stop, skip_group_check=True)

        def fm_block(pe, o, s, c0, stride, kts, k0, first, last):
            for k in range(kts):
                c = k * stride + c0
                mm = three(pe, o, whi[:, s, c:c + P], wlo[:, s, c:c + P], hhi[:, k0 + k, :], hlo[:, k0 + k, :],
                           first and k == 0, last and k == kts - 1)
            return mm

        def tm_pass(pe, s, st, first, last):
            for c in range(NT):
                h, l = shi[:, st, c * P:(c + 1) * P], slo[:, st, c * P:(c + 1) * P]
                for n in range(4):
                    pe.matmul(ps[:, 4 * c + n, :], h, whi[:, s, n * 512:(n + 1) * 512], start=first, stop=False,
                              skip_group_check=True)
                for n in range(4):
                    pe.matmul(ps[:, 4 * c + n, :], h, wlo[:, s, n * 512:(n + 1) * 512], start=False, stop=False,
                              skip_group_check=True)
                for n in range(4):
                    mm = pe.matmul(ps[:, 4 * c + n, :], l, whi[:, s, n * 512:(n + 1) * 512], start=False, stop=last,
                                   skip_group_check=True)
            return mm

        def stage_hi(act, src, m0, mpr, jm, i):
            if m0 + jm >= 2 or not isinstance(i, int):
                act.wait_ge(w_used, i * mpr + (m0 + jm - 1))
            act.activation(shi[:, (m0 + jm) % 2, :], src, ACT.Identity)

        def stage_lo(dve, src, m0, mpr, jm, i):
            dve.wait_ge(hi_ready, i * mpr + (m0 + jm + 1))
            dve.tensor_tensor(slo[:, (m0 + jm) % 2, :], src, shi[:, (m0 + jm) % 2, :].bitcast(F32), ALU.subtract)

        def newton(ch, dve, y, x, t):
            ch.link(dve.tensor_scalar(y.bitcast(I32), x.bitcast(I32), -0.5, RSQRT_SEED, ALU.mult, ALU.add))
            for _ in range(3):
                ch.link(dve.tensor_tensor(t, y, y, ALU.mult))
                ch.link(dve.scalar_tensor_tensor(out=t, in0=t, scalar=-0.5, in1=x, op0=ALU.mult, op1=ALU.mult))
                ch.link(dve.scalar_tensor_tensor(out=y, in0=t, scalar=1.5, in1=y, op0=ALU.add, op1=ALU.mult))

        def bc(v, n):
            return v.unsqueeze(2).to_broadcast([P, v.shape[1], n])

        def rep(v, n):
            return v.unsqueeze(1).to_broadcast([P, n, v.shape[1]])

        def norm_col(which, layer):
            at = (which * 2 + layer) * KT
            return normc[:, at:at + KT]

        SUB = [dict(layer=s // 2, pre=0 if s % 2 == 0 else 2, post=1 if s % 2 == 0 else 3,
                    sh=0 if s % 2 == 0 else 3, sc=1 if s % 2 == 0 else 4, gt=2 if s % 2 == 0 else 5)
               for s in range(4)]
        gwrow_of = [gwrow_mix, gwrow_ffn, gwrow_mix, gwrow_ffn]

        def mod_cols(layer, chunk):
            return modc[:, layer, chunk * KT:(chunk + 1) * KT]

        FINALS = [(0, [0, 1], macc), (0, [2, 3], macc), (0, [4, 5], macc), (1, [0, 1, 2, 3], macc4),
                  (1, [4, 5], macc4)]
        H_HI = [0, KT, 2 * KT, 3 * KT + 2]
        mod_ends = [n_ab, n_dout, n_gu0, n_dn0, n_sin]

        block = ctx.enter_context(nc.Block())

        @block.sync
        def _(sp):
            rows = pin
            sp.dma_start(xbuf, a["x"][0].rearrange("(c p) n -> p c n", p=P)).then_inc(x_landed, 16)
            for n, name in enumerate(("norm_pre_mix", "norm_post_mix", "norm_pre_ffn", "norm_post_ffn")):
                sp.dma_start(rows[32 * n:32 * n + 32, 0, :],
                             a[name].rearrange("l (k p) -> (l k) p", p=P)).then_inc(params_in, 16)
            mb = a["mod_b"].rearrange("l (k p) -> (l k) p", p=P)
            sp.dma_start(rows[0:96, 1, :], mb[0:96, :]).then_inc(params_in, 16)
            sp.dma_start(rows[0:96, 2, :], mb[96:192, :]).then_inc(params_in, 16)
            sp.dma_start(rows[0:16, 3, :], a["c"].rearrange("b (k p) -> (b k) p", p=P)).then_inc(params_in, 16)
            sp.dma_start(rows[16:32, 3, :], a["s5_d"].rearrange("b (k p) -> (b k) p", p=P)).then_inc(params_in, 16)
            sp.dma_start(rows[32:33, 3, :], a["dn_norm_w"]).then_inc(params_in, 16)
            cw = a["dn_conv_w"].rearrange("l j (t p) -> (l j t) p", p=P)
            sp.dma_start(rows[:, 4, :], cw[0:128, :]).then_inc(params_in, 16)
            sp.dma_start(rows[:, 5, :], cw[128:256, :]).then_inc(params_in, 16)
            sp.dma_start(rows[0:64, 6, :], cw[256:320, :]).then_inc(params_in, 16)
            sp.wait_ge(consts_ready, 1)
            for d in range(2):
                r = 64 * d + 32
                sp.dma_start(small[r:r + 32, 0:1], a["dn_a_log"][0, d, :].rearrange("(h o) -> h o", o=1)).then_inc(params_in, 16)
                sp.dma_start(small[r:r + 32, 1:2], a["dn_dt_bias"][0, d, :].rearrange("(h o) -> h o", o=1)).then_inc(params_in, 16)
            for j in range(2):
                load_mod(sp, 0, 0, 2, j, 0, 0, j)
            with sp.Fori(0, KT - 1) as k:
                for j in range(2):
                    load_mod(sp, 2, k, 2, j, 0, k + 1, j)
            w_in = a["dn_w_in"][0]
            load_cols(sp, n_ab, 0, 1, 0, w_in, 0, KT, ABOFF, P)

            def head_tiles(h):
                load_cols(sp, n_head, h, PER_HEAD, 0, w_in, 0, KT, QOFF + h * P, P)
                load_cols(sp, n_head, h, PER_HEAD, 1, w_in, 0, KT, KOFF + h * P, P)
                for j in range(2):
                    load_cols(sp, n_head, h, PER_HEAD, 2 + j, w_in, 8 * j, 8, VOFF + h * 256, 256)
                for j in range(2):
                    load_cols(sp, n_head, h, PER_HEAD, 4 + j, w_in, 8 * j, 8, ZOFF + h * 256, 256)
                for j in range(2):
                    load_mod(sp, n_head, h, PER_HEAD, 6 + j, 0, h, 2 + j)

            with sp.Fori(0, KH) as h:
                head_tiles(h)
            def load_x(s):
                src = a["x"][0] if s == 0 else x_dram[s - 1]
                sp.wait_ge(w_used, post_m[s])
                if s > 0:
                    sp.wait_ge(x_stored, 16 * s)
                sp.dma_start(xbuf, src.rearrange("(c p) n -> p c n", p=P)).then_inc(x_landed, 16)

            def store_x(s):
                sp.wait_ge(x_new, s + 1)
                dst = out[0] if s == 3 else x_dram[s]
                sp.dma_start(dst.rearrange("(c p) n -> p c n", p=P), xbuf).then_inc(x_stored, 16)

            def gateup(n0, layer, loops):
                wg, wu = a["ffn_w_gate"][layer], a["ffn_w_up"][layer]
                lm, lp = loops

                def pair(nb, i, per, j0, col):
                    for w, j in ((wg, 0), (wg, 1), (wu, 2), (wu, 3)):
                        load_cols(sp, nb, i, per, j0 + j, w, 8 * (j % 2), 8, col, 256)

                if lm:
                    with sp.Fori(0, lm) as i:
                        for r in range(2):
                            pair(n0, i, 16, 8 * r, i * 512 + r * 256)
                            for j in range(4):
                                load_mod(sp, n0, i, 16, 8 * r + 4 + j, 1, i * 2 + r, j)
                n1 = n0 + 16 * lm
                with sp.Fori(0, lp) as i:
                    for r in range(2):
                        pair(n1, i, 8, 4 * r, i * 512 + (r * 256 + lm * 512))

            def down(n0, w, kts, lm, layer):
                if lm:
                    with sp.Fori(0, lm) as i:
                        for r in range(2):
                            for j in range(2):
                                load_rows(sp, n0, i, 8, 4 * r + j, w, i * (4 * P) + (2 * r + j) * P)
                            for j in range(2):
                                load_mod(sp, n0, i, 8, 4 * r + 2 + j, layer, i * 2 + r, 4 + j)
                n1 = n0 + 8 * lm
                if kts // 4 > lm:
                    with sp.Fori(0, kts // 4 - lm) as i:
                        for j in range(4):
                            load_rows(sp, n1, i, 4, j, w, i * (4 * P) + (j + 4 * lm) * P)

            down(n_dout, a["dn_w_out"][0], VH, LOOPM, 0)
            load_x(0)
            store_x(0)
            gateup(n_gu0, 0, (LOOPM, 3))
            down(n_dn0, a["ffn_w_down"][0], FT, LOOPM, 1)
            load_x(1)
            store_x(1)

            def square(n0, w):
                with sp.Fori(0, 4) as i:
                    for r in range(2):
                        for j in range(2):
                            load_cols(sp, n0, i, 4, 2 * r + j, w, 8 * j, 8, i * 512 + r * 256, 256)

            square(n_sin, a["s5_w_in"][0])
            sp.wait_ge(h_ready, 3)
            sp.wait_ge(mod_ps, 5)
            for r, name in enumerate(("s5_b_re", "s5_b_im")):
                for d in range(2):
                    sp.dma_start(bnat[:, r, d * GP * Q:(d + 1) * GP * Q].rearrange("p (g c) -> p g c", c=Q),
                                 a[name][0, d].rearrange("(g e) p c -> (e p) g c", e=2)).then_inc(s5_in, 16)
            for r, name in enumerate(("s5_c_re", "s5_c_im")):
                for d in range(2):
                    sp.dma_start(cnat[:, r, d, :, :],
                                 a[name][0, d].rearrange("(j g) c p -> (g c) j p", g=8)).then_inc(s5_in, 16)
            sp.dma_start(s5w[:, 0, :], a["s5_lam_re"][0].rearrange("d (g e) p -> (d g) (e p)", e=2)).then_inc(s5_in, 16)
            sp.dma_start(s5w[:, 1, :], a["s5_lam_im"][0].rearrange("d (g e) p -> (d g) (e p)", e=2)).then_inc(s5_in, 16)
            sp.dma_start(s5w[:, 2, 0:2], a["s5_log_step"][0].rearrange("d (g e) -> (d g) e", e=2)).then_inc(s5_in, 16)
            square(n_glu, a["s5_w_glu"][0])
            down(n_sout, a["s5_w_out"][0], KT, 0, 1)
            load_x(2)
            store_x(2)
            gateup(n_gu1, 1, (0, 11))
            down(n_dn1, a["ffn_w_down"][1], FT, 0, 1)
            load_x(3)
            store_x(3)
            sp.wait_ge(x_stored, 64)


        QK_BANK, V_BANK, Z_BANK, K_BANK, XY, TT = 0, 1, 2, 3, (4, 5), (6, 7)

        def changed(v, l, d):
            return v.rearrange("p u (n t b) -> p u n t b", t=2, b=2 << l)[:, :, :, d, :]

        def at_level(h, l, d):
            return h * (2 * LV) + (2 * l + d + 1)

        def plan(n0, m0, kts, lm):
            out_, i, its = [], 0, kts // 4
            while i < its:
                per = 8 if i < lm else 4
                end = i + 1 if i in (0, its - 1) else (min(lm, its - 1) if i < lm else its - 1)
                out_.append((n0, m0 + 4 * i, 4 * i, end - i, per, i == 0, end == its))
                n0 += per * (end - i)
                i = end
            return out_

        def raw_at(per, j):
            return j if per == 4 else 4 * (j // 2) + j % 2

        def run(eng, trips, body):
            if trips == 1:
                body(0)
            else:
                with eng.Fori(0, trips) as i:
                    body(i)

        @block.tensor
        def _(pe):
            def finish_mod(f):
                layer, chunks, acc = FINALS[f]
                pe.wait_ge(raw_used, mod_ends[f])
                for n in range(len(chunks)):
                    for k in range(KT):
                        mm = pe.matmul(ps[:, 7, n * KT + k:n * KT + k + 1], acc[:, n, k * P:(k + 1) * P],
                                       ones[:, 0:1], start=True, stop=True)
                mm.then_inc(mod_ps, 1)

            def gate_rows(s):
                for g in range(4):
                    pe.wait_ge(diag_ready, 4 * s + g + 1)
                    pe.matmul(ps[:, g, :], ones, diag[:, g, :, :].rearrange("p u i -> p (u i)"),
                              start=True, stop=True).then_inc(gw_ps, 1)

            def pre_norm(s):
                pe.wait_ge(xn_ready, 2 * s + 2)
                for k in range(KT):
                    for c in range(NT):
                        mm = pe.transpose(ps[:, k // 2, (k % 2) * T + c * P:(k % 2) * T + (c + 1) * P],
                                          xn[:, c, k * P:(k + 1) * P], ident)
                    if k % 2:
                        mm.then_inc(xnT_ps, 1)

            def token_major(n0, m0, kts, lm):
                for nb, mb, _, trips, per, first, last in plan(n0, m0, kts, lm):
                    def body(i):
                        for j in range(4):
                            split_ready(pe, nb, per, raw_at(per, j), mb, 4, j, i)
                            tm_pass(pe, (mb + j) % 2, (mb + j) % 2, first and j == 0,
                                    last and j == 3).then_inc(w_used, 1)
                    run(pe, trips, body)

            def half_tile(h, k, prev):
                j, half = k // 2, k % 2
                s = (m_head + j) % 2
                if half == 0:
                    split_ready(pe, n_head, PER_HEAD, j, m_head, 6, j, h)
                if j < 2:
                    if k == 0 and prev:
                        pe.wait_ge(cbuf_ready, h * 2 - 1)
                    mm = fm_block(pe, ps[:, QK_BANK, j * T:(j + 1) * T], s, half * 8 * P, P, 8, 8 * half,
                                  half == 0, half == 1)
                elif j < 4:
                    if k == 4 and prev:
                        pe.wait_ge(cbuf_ready, h * 2)
                    mm = fm_block(pe, ps[:, V_BANK, half * T:(half + 1) * T], s, half * P, 2 * P, 8, 8 * (j - 2),
                                  j == 2 and half == 0, j == 3)
                else:
                    if k == 8 and prev:
                        pe.wait_ge(zg_ready, h)
                    for kt in range(8):
                        kk = 8 * (j - 4) + kt
                        mm = three(pe, ps[:, Z_BANK, half * T:(half + 1) * T],
                                   hhi[:, kk, half * P:(half + 1) * P], hlo[:, kk, half * P:(half + 1) * P],
                                   whi[:, s, kt * 2 * P:(kt + 1) * 2 * P], wlo[:, s, kt * 2 * P:(kt + 1) * 2 * P],
                                   j == 4 and half == 0 and kt == 0, j == 5 and kt == 7)
                if half == 1:
                    mm.then_inc(w_used, 1)

            def core(h, nxt):
                nxt(0)
                nxt(1)
                nxt(2)
                pe.wait_ge(act_done, h + 1)
                for u in range(4):
                    pe.transpose(ps[:, TT[0], u * P:(u + 1) * P], yact[:, u * P:(u + 1) * P], ident)
                for u in range(4):
                    mm = pe.transpose(ps[:, TT[1], u * P:(u + 1) * P], yact[:, (4 + u) * P:(5 + u) * P], ident)
                mm.then_inc(tok_ps, 1)
                nxt(3)
                pe.wait_ge(qkn_ready, h + 1)
                for u in range(4):
                    mm = pe.transpose(ps[:, XY[0], u * P:(u + 1) * P], qkn[:, u, :], ident)
                mm.then_inc(qkT_ps, 1)
                nxt(4)
                pe.wait_ge(qkT_ready, h + 1)
                for m in range(2):
                    for c in range(NT):
                        mm = pe.matmul(ps[:, K_BANK, (2 * m + c) * P:(2 * m + c + 1) * P], qkT[:, 2 + c, :],
                                       qkT[:, 2 - 2 * m + c, :], start=True, stop=True)
                mm.then_inc(kk_ps, 1)
                nxt(5)
                for d in range(2):
                    pe.wait_ge(s0_ready, h * 2 + (d + 1))
                    pe.wait_ge(vb_ready, h + 1)
                    for u in range(4):
                        mm = pe.transpose(ps[:, TT[d], u * P:(u + 1) * P], Sm[:, 4 * d + u, :], ident)
                    mm.then_inc(t0_ps, 1)
                for l in range(LV):
                    for d in range(2):
                        if l == 0:
                            pe.wait_ge(t0_ready, h * 2 + (d + 1))
                        else:
                            pe.wait_ge(t_ready, at_level(h, l - 1, d))
                        for u in range(4):
                            mm = pe.matmul(ps[:, XY[d], u * 64:(u + 1) * 64], Bm[:, 4 * d + u, :],
                                           changed(Tm[:, 4 * d + u:4 * d + u + 1, :], l, d)[:, 0],
                                           start=True, stop=True)
                        mm.then_inc(x_ps, 1)
                    for d in range(2):
                        pe.wait_ge(xm_ready, at_level(h, l, d))
                        if l > 0:
                            pe.wait_ge(s_ready, at_level(h, l - 1, d))
                        for u in range(4):
                            mm = pe.matmul(ps[:, XY[d], 256 + u * 64:256 + (u + 1) * 64], Sm[:, 4 * d + u, :],
                                           Xm[:, d, u, :], start=True, stop=True)
                        mm.then_inc(y_ps, 1)
                    for d in range(2):
                        pe.wait_ge(t_ready, at_level(h, l, d))
                        for u in range(4):
                            mm = pe.transpose(ps[:, TT[d], u * P:(u + 1) * P], Tm[:, 4 * d + u, :], ident)
                        mm.then_inc(tt_ps, 1)
                    nxt(6 + l)
                for d in range(2):
                    pe.wait_ge(s_ready, at_level(h, LV - 1, d))
                    for v in range(2):
                        mm = pe.matmul(ps[:, XY[d], v * P:(v + 1) * P], Sm[:, 4 * d + 2 * v + d, :],
                                       Vb[:, 4 * d + 2 * v + d, :], start=True, stop=True)
                    mm.then_inc(u0_ps, 1)
                pe.wait_ge(ktail_ready, h + 1)
                for d in range(2):
                    pe.wait_ge(u0_ready, h * 2 + (d + 1))
                    for v in range(2):
                        mm = pe.matmul(ps[:, TT[d], v * P:(v + 1) * P], Kt[:, d, v, :],
                                       Vn[:, 4 * d + 2 * v + d, :], start=True, stop=True)
                    mm.then_inc(st_ps, 1)
                for d in range(2):
                    pe.wait_ge(st_ready, h * 2 + (d + 1))
                    state = Ssb[:, d, :, :].rearrange("p v i -> p (v i)")
                    pe.matmul(ps[:, XY[d], 256:512], qkT[:, 3 - d, :], state, start=True, stop=True)\
                        .then_inc(ks_ps, 1)
                    pe.matmul(ps[:, TT[d], 256:512], qkT[:, 1 - d, :], state, start=True, stop=True)\
                        .then_inc(ks_ps, 1)
                for d in range(2):
                    pe.wait_ge(r1_ready, h * 2 + (d + 1))
                    for v in range(2):
                        mm = pe.matmul(ps[:, XY[d], v * P:(v + 1) * P], Sm[:, 4 * d + 2 * v + 1 - d, :],
                                       R1[:, d, v, :], start=True, stop=True)
                    mm.then_inc(v1_ps, 1)
                pe.wait_ge(aqk_ready, h * 2 + 2)
                pe.wait_ge(v1_ready, h * 2 + 2)
                for u in range(4):
                    for d in range(2):
                        mm = pe.matmul(ps[:, K_BANK, u * P:(u + 1) * P], Aqk[:, 4 * d + u, :], Vn[:, 4 * d + u, :],
                                       start=d == 0, stop=d == 1)
                mm.then_inc(o_ps, 1)
                pe.wait_ge(og_ready, h + 1)
                for u in range(4):
                    mm = pe.transpose(ps[:, TT[0], u * P:(u + 1) * P], Osb[:, u, :], ident)
                mm.then_inc(oT_ps, 1)

            def pair_gemm(nb, nper, jn, mb, mper, jm, i, bank):
                for j in range(2):
                    split_ready(pe, nb, nper, jn + j, mb, mper, jm + j, i)
                    for b in range(2):
                        mm = fm_block(pe, ps[:, bank, b * T:(b + 1) * T], (mb + jm + j) % 2, b * P, 2 * P, 8, 8 * j,
                                      j == 0 and b == 0, j == 1)
                    mm.then_inc(w_used, 1)

            def gateup(n0, m0, q0, lm, lp):
                def pairs(i, nb, nper, mb, q):
                    for r in range(2):
                        jn = (nper // 2) * r
                        pe.wait_ge(gate_used, i * 2 + (q + r + 1))
                        pair_gemm(nb, nper, jn, mb, 8, 4 * r, i, r)
                        pe.wait_ge(hid_ready, i * 2 + (q + r + 1))
                        pair_gemm(nb, nper, jn + 2, mb, 8, 4 * r + 2, i, 2 + r)
                if lm:
                    with pe.Fori(0, lm) as i:
                        pairs(i, n0, 16, m0, q0)
                with pe.Fori(0, lp) as i:
                    pairs(i, n0 + 16 * lm, 8, m0 + 8 * lm, q0 + 2 * lm)

            def square(n0, m0, q0):
                with pe.Fori(0, 4) as i:
                    for r in range(2):
                        pe.wait_ge(fm_done, i * 2 + (q0 + r + 1))
                        pair_gemm(n0, 4, 2 * r, m0, 4, 2 * r, i, r)

            pe.wait_ge(consts_ready, 3)
            pe.wait_ge(params_in, 16 * 16)
            for n, rows in enumerate((128, 96, 96, 33, 128, 128, 64)):
                mm = pe.transpose(ps[:, n // 4, (n % 4) * P:(n % 4) * P + rows], pin[0:rows, n, :],
                                  ident[0:rows, 0:rows])
            mm.then_inc(params_T, 1)
            finish_mod(0)
            pe.wait_ge(mod_ready, 1)
            pre_norm(0)
            pe.wait_ge(h_ready, 1)
            split_ready(pe, n_ab, 1, 0, m_ab, 1, 0, 0)
            fm_block(pe, ps[:, 4, 0:T], m_ab % 2, 0, P, KT, 0, True, True).then_inc(w_used, 1)
            pe.wait_ge(ab_dve, 3)
            for n in range(4):
                src = abw[:, 1 if n < 2 else 2, (n % 2) * P:(n % 2 + 1) * P]
                mm = pe.transpose(ps[:, 5, n * P:(n + 1) * P], src, ident)
            mm.then_inc(gT_ps, 1)
            pe.wait_ge(tbl_ready, 1)
            for k in range(12):
                half_tile(0, k, False)
            with pe.Fori(0, KH - 1) as h:
                core(h, lambda k: half_tile(h + 1, k, True))
            core(KH - 1, lambda k: None)
            pe.wait_ge(oT_ready, KH)
            finish_mod(1)
            gate_rows(0)
            pe.wait_ge(gw_ready, 4)
            pe.wait_ge(mod_ready, 2)
            token_major(n_dout, m_dout, VH, LOOPM)
            pe.wait_ge(x_new, 1)
            finish_mod(2)
            pe.wait_ge(mod_ready, 3)
            pre_norm(1)
            pe.wait_ge(h_ready, 2)
            gate_rows(1)
            pe.wait_ge(gw_ready, 8)
            gateup(n_gu0, m_gu0, 0, LOOPM, 3)
            finish_mod(3)
            pe.wait_ge(mod_ready, 4)
            pe.wait_ge(hid_ready, 2 + FT // 2)
            token_major(n_dn0, m_dn0, FT, LOOPM)
            pe.wait_ge(x_new, 2)
            finish_mod(4)
            pe.wait_ge(mod_ready, 5)
            pre_norm(2)
            pe.wait_ge(h_ready, 3)
            square(n_sin, m_sin, 0)

            pe.wait_ge(s5_dve, 1)
            for n in range(4):
                mm = pe.transpose(ps[:, 2, n * P:(n + 1) * P], s5w[:, S5OUT[n], :], ident)
            mm.then_inc(s5_psT, 1)
            pe.wait_ge(fm_done, 2 + 8)

            def s5_tile(j):
                if True:
                    pe.wait_ge(bx_ready, j + 1)
                    pe.wait_ge(bT_ready, j)
                    for n in range(4):
                        pe.transpose(ps[:, 0, n * P:(n + 1) * P], bx[:, n, :], ident)
                    pe.wait_ge(cdup_ready, j + 1)
                    pe.wait_ge(cj_ready, j)
                    for n in range(4):
                        mm = pe.transpose(ps[:, 1, n * P:(n + 1) * P], cdup[:, n, :], ident)
                    mm.then_inc(bcT_ps, 1)

                def bu(q):
                    g, d = q // 2, q % 2
                    if q == 0:
                        pe.wait_ge(bT_ready, j + 1)
                        pe.wait_ge(uj_ready, j + 1)
                    pe.wait_ge(t_prod, j * 8 + (q - 1)) if q >= 1 else None
                    for r in range(2):
                        mm = pe.matmul(ps[:, 2 + q % 2, r * T:(r + 1) * T], bT[32 * g:32 * g + 32, 2 * d + r, :],
                                       uj[32 * g:32 * g + 32, :], start=True, stop=True)
                    mm.then_inc(bu_ps, 1)

                def y(q):
                    g, d = q // 2, q % 2
                    if q == 0:
                        pe.wait_ge(cj_ready, j + 1)
                        pe.wait_ge(ysum_ready, j)
                    o = ps[32 * g:32 * g + 32, 4, 0:T]
                    pe.wait_ge(pcos_ready, j * 8 + (q + 1))
                    for r in range(2):
                        pe.matmul(o, cj[:, r, (2 * d + r) * P + 32 * g:(2 * d + r) * P + 32 * g + 32], pcos[:, r, :],
                                  start=d == 0 and r == 0, stop=False)
                    pe.wait_ge(psin_ready, j * 8 + (q + 1))
                    for r in range(2):
                        mm = pe.matmul(o, cj[:, 1 - r, (2 * d + r) * P + 32 * g:(2 * d + r) * P + 32 * g + 32],
                                       psin[:, r, :], start=False, stop=d == 1 and r == 1)
                    mm.then_inc(ymm, 1)

                for q in range(8):
                    bu(q)
                    if q >= 1:
                        y(q - 1)
                y(7)

            pe.wait_ge(s5_ready, 1)
            with pe.Fori(0, NJ) as j:
                s5_tile(j)
            gate_rows(2)
            pe.wait_ge(gw_ready, 12)
            pe.wait_ge(glu_h, 2)
            square(n_glu, m_glu, 8)
            pe.wait_ge(fm_done, 2 + 16)
            token_major(n_sout, m_sout, KT, 0)
            pe.wait_ge(x_new, 3)
            pre_norm(3)
            pe.wait_ge(h_ready, 4)
            gate_rows(3)
            pe.wait_ge(gw_ready, 16)
            gateup(n_gu1, m_gu1, FT // 2, 0, FT // 4)
            pe.wait_ge(hid_ready, 2 + FT)
            token_major(n_dn1, m_dn1, FT, 0)

        @block.gpsimd
        def _(pool):
            ch = Chain(pool, pools)

            def select(view, pattern, base, cm, op=ALU.is_ge, fill=0.0):
                ch.link(pool.affine_select(out=view, in_=view, compare_op=op, fill=fill, base=base,
                                           pattern=pattern, channel_multiplier=cm))

            pool.memset(small, 0.0).then_inc(consts_ready, 1)
            ch.link(pool.memset(ones, 1.0))
            ch.link(pool.memset(ident, 0.0))
            select(ident, [[-1, P]], 0, 1, ALU.not_equal, 1.0)
            pool.wait_ge(pools, 3)
            pool.memset(macc, 0.0).then_inc(macc_zero, 1)
            ch.link(pool.memset(mkq[:, :, 0, :], 1.0))
            ch.link(pool.memset(mkq[:, :, 1, :], DK_SCALE))
            for d in range(2):
                sg = 1 if d == 0 else -1
                select(mkq[:, d, 0, :], [[sg, P]], -1, -sg)
                select(mkq[:, d, 1, :], [[sg, P]], 0, -sg)
            ch.link(pool.memset(m1, 0.0))
            for d in range(2):
                v = m1[:, d, :].rearrange("p (a r) -> p a r", r=2)[:, :, 1 - d]
                select(v, [[-2, P // 2]], -d, 1, ALU.not_equal, -1.0)
            ch.link(pool.memset(mlv, -1.0))
            for l in range(LV):
                b = 2 << l
                for d in range(2):
                    v = mlv[:, l, d, :].rearrange("p (n b) -> p n b", b=b)
                    select(v, [[-2 * b, 64 // b], [0, b]], -(1 - d) * b, 1)
                    select(v, [[2 * b, 64 // b], [0, b]], (2 - d) * b - 1, -1)
            pool.sem_inc(consts_ready, 2)
            pool.wait_ge(ab_dve, 3)
            for d in range(2):
                pool.dma_start(g_rows[d * VH:(d + 1) * VH, :], abw[64 * d + 32:64 * d + 64, 1, :]).then_inc(rows_stored, 16)
                pool.dma_start(b_rows[d * VH:(d + 1) * VH, :], abw[64 * d:64 * d + 32, 2, :]).then_inc(rows_stored, 16)
            pool.wait_ge(mod_ps, 1)
            pool.memset(macc, 0.0).then_inc(macc_zero, 1)
            pool.wait_ge(rows_stored, 64)

            def core(h, later):
                if later:
                    pool.wait_ge(oss_ready, h)
                    pool.wait_ge(og_ready, h)
                    pool.wait_ge(oT_ps, h)
                for d in range(2):
                    for dst, src in ((grow, g_rows), (brow, b_rows)):
                        pool.dma_start(dst[:, 4 * d:4 * d + 4, :].rearrange("p (v c) i -> p v (c i)", v=2),
                                       src[ds(h * 2 + d * VH, 2), :].partition_broadcast(P)).then_inc(rows_landed, 16)
                if later:
                    pool.wait_ge(tt_ps, h * (2 * LV))
                for d in range(2):
                    pool.wait_ge(e_ready, h * 2 + (d + 1))
                    pool.wait_ge(rows_landed, h * 64 + 64)
                    pool.tensor_tensor(Bm[:, 4 * d:4 * d + 4, :], eD[:, d * 512:(d + 1) * 512].rearrange("p (u i) -> p u i", u=4),
                                       brow[:, 4 * d:4 * d + 4, :], ALU.mult).then_inc(eb_ready, 1)
                for d in range(2):
                    pool.wait_ge(km_ready, h + 1)
                    for v in range(2):
                        mm = pool.tensor_tensor(Aqk[:, 4 * d + 2 * v:4 * d + 2 * v + 2, :], km[:, d, 1, :, :],
                                                eD[:, d * 512 + v * 256:d * 512 + (v + 1) * 256].rearrange("p (u i) -> p u i", u=2),
                                                ALU.mult)
                    mm.then_inc(aqk_ready, 1)

            core(0, False)
            with pool.Fori(0, KH - 1) as h:
                core(h + 1, True)
            pool.wait_ge(mod_ps, 2)
            pool.memset(macc, 0.0).then_inc(macc_zero, 1)
            pool.wait_ge(gw_ps, 8)
            pool.wait_ge(mod_ps, 3)
            pool.memset(macc4, 0.0).then_inc(macc_zero, 1)
            pool.wait_ge(mod_ps, 4)
            pool.memset(macc4[:, 0:2, :], 0.0).then_inc(macc_zero, 1)

            pool.wait_ge(s5_ready, 1)
            ch.link(pool.memset(gmask, 0.0))
            for sgn in range(2):
                for e in range(2):
                    v = gmask[64 * e:64 * e + 64, sgn, :].rearrange("p (g e c) -> p g e c", g=4, e=2)[:, :, e, :]
                    ch.link(pool.memset(v, 1.0 if sgn == 0 else -1.0))
            ch.link(pool.iota(iota, pattern=[[1, T]], base=0, channel_multiplier=0,
                              allow_small_or_imprecise_dtypes=True))
            pool.sem_inc(s5_act, 1)
            with pool.Fori(0, NJ) as j:
                pool.wait_ge(bcT_ps, j)
                for n in range(4):
                    d, r = n // 2, n % 2
                    src = bnat[:, r, :].rearrange("p (g c) -> p g c", c=Q)[:, ds(j * 4 + d * GP, 4), :]
                    m = pool.tensor_tensor(bx[:, n, :].rearrange("p (g e c) -> p g e c", g=4, e=2),
                                           src.unsqueeze(2).to_broadcast([P, 4, 2, Q]),
                                           gmask[:, 0, :].rearrange("p (g e c) -> p g e c", g=4, e=2), ALU.mult)
                m.then_inc(bx_ready, 1)
                for n in range(4):
                    d, r = n // 2, n % 2
                    for e in range(2):
                        m = pool.tensor_copy(cdup[:, n, e * 64:(e + 1) * 64],
                                             cnat[:, r, d, ds(j, 1), :].rearrange("p o s -> p (o s)"))
                m.then_inc(cdup_ready, 1)
                pool.wait_ge(ysum_ready, j)
                pool.tensor_copy(uj, uT[:, ds(j, 1), :].rearrange("p o t -> p (o t)")).then_inc(uj_ready, 1)
                for q in range(8):
                    pool.wait_ge(t_prod, j * 8 + (q + 1))
                    pool.wait_ge(z_ready, j * 8 + q)
                    pool.tensor_tensor(zin, tc_, ts_, ALU.add).then_inc(zin_ready, 1)
                    pool.wait_ge(z_ready, j * 8 + (q + 1))
                    pool.wait_ge(ymm, j * 8 + q)
                    pool.tensor_tensor(psin, trig[:, q % 2, 1:3, :], zst[:, ::-1, :], ALU.mult).then_inc(psin_ready, 1)

        @block.scalar
        def _(act):
            ch = Chain(act, acts)
            IDT = ACT.Identity

            def post(s):
                act.wait_ge(w_used, post_m[s])
                for n in range(8):
                    m = act.activation(ptmp[:, n // 4, n % 4 * 512:(n % 4 + 1) * 512], ps[:, n, :], ACT.Square, accum_out=small[:, 8 + n:9 + n])
                m.then_inc(ss_out, 1)

            def pre_norm(s):
                act.wait_ge(x_landed, 16) if s == 0 else act.wait_ge(x_new, s)
                for c in range(NT):
                    m = act.activation(xn[:, c, :], xbuf[:, c, :], ACT.Square, accum_out=small[:, 24 + c:25 + c])
                m.then_inc(ss_x, 1)
                act.wait_ge(rstd_x, s + 1)
                for c in range(NT):
                    act.activation(xn[:, c, :], xbuf[:, c, :], IDT, scale=small[:, 28 + c:29 + c]).then_inc(xn_ready, 1)
                layer, sh = SUB[s]["layer"], SUB[s]["sh"]
                for k in range(KT):
                    if k % 2 == 0:
                        act.wait_ge(xnT_ps, 8 * s + k // 2 + 1)
                    act.activation(hhi[:, k, :], ps[:, k // 2, (k % 2) * T:(k % 2 + 1) * T], IDT,
                                   scale=acol[:, k:k + 1],
                                   bias=mod_cols(layer, sh)[:, k:k + 1]).then_inc(h_hi, 1)

            def stream(n0, m0, kts, lm, src):
                for nb, mb, kb_, trips, per, first, last in plan(n0, m0, kts, lm):
                    def body(i):
                        for j in range(4):
                            stage_hi(act, src[:, ds(i * 4 + (kb_ + j), 1), :].rearrange("p o t -> p (o t)"),
                                     mb, 4, j, i)
                            split_hi(act, nb, per, raw_at(per, j), mb, 4, j, i)
                    run(act, trips, body)

            def gate_tanh_of(q, r, m_done):
                act.wait_ge(w_used, m_done)
                act.wait_ge(hid_ready, q + 1)
                act.activation(fth[:, r, :], ps[:, r, :], ACT.Tanh, scale=0.5).then_inc(gate_tanh, 1)

            def gateup(n0, m0, q0, lm, lp):
                def pairs(i, nb, nper, mb, q):
                    for r in range(2):
                        jn = (nper // 2) * r
                        for j in range(4):
                            split_hi(act, nb, nper, jn + j, mb, 8, 4 * r + j, i)
                            if j == 3:
                                gate_tanh_of(i * 2 + (q + r), r, i * 8 + (mb + 4 * r + 2))
                if lm:
                    with act.Fori(0, lm) as i:
                        pairs(i, n0, 16, m0, q0)
                with act.Fori(0, lp) as i:
                    pairs(i, n0 + 16 * lm, 8, m0 + 8 * lm, q0 + 2 * lm)

            def head_hi(h, j):
                split_hi(act, n_head, PER_HEAD, j, m_head, 6, j, h)

            def core(h, nxt):
                act.wait_ge(w_used, h * 6 + (m_head + 2))
                act.wait_ge(o_ps, h)
                for edge in (slice(0, PAD), slice(PAD + T, 2 * PAD + T)):
                    act.activation(cbuf[:, :, edge], ones[:, 0:4 * PAD].rearrange("p (t n) -> p t n", t=4), IDT,
                                   scale=0.0)
                act.activation(cbuf[:, 0:2, PAD:PAD + T], ps[:, QK_BANK, :].rearrange("p (t n) -> p t n", t=2),
                               IDT).then_inc(cbuf_ready, 1)
                act.wait_ge(w_used, h * 6 + (m_head + 4))
                act.activation(cbuf[:, 2:4, PAD:PAD + T], ps[:, V_BANK, :].rearrange("p (t n) -> p t n", t=2),
                               IDT).then_inc(cbuf_ready, 1)
                nxt(0)
                act.wait_ge(conv_done, h + 1)
                act.activation(eD, yact, ACT.Tanh, scale=0.5).then_inc(silu_tanh, 1)
                act.wait_ge(w_used, h * 6 + (m_head + 6))
                act.activation(zth.rearrange("p u i -> p (u i)"), ps[:, Z_BANK, :], ACT.Tanh, scale=0.5).then_inc(z_tanh, 1)
                nxt(1)
                act.wait_ge(tok_ps, h + 1)
                act.wait_ge(oss_ready, h)
                for u in range(4):
                    m = act.activation(junk[:, u * P:(u + 1) * P], ps[:, TT[0], u * P:(u + 1) * P], ACT.Square,
                                       accum_out=small[:, 32 + u:33 + u])
                m.then_inc(ss_ready, 1)
                nxt(2)
                act.wait_ge(qkT_ps, h + 1)
                act.activation(qkT.rearrange("p u i -> p (u i)"), ps[:, XY[0], :], IDT).then_inc(qkT_ready, 1)
                for d in range(2):
                    act.wait_ge(de_ready, h + 1)
                    act.activation(eD[:, d * 512:(d + 1) * 512], eD[:, d * 512:(d + 1) * 512], ACT.Exp).then_inc(e_ready, 1)
                act.wait_ge(e_ready, h * 2 + 2)
                for d in range(2):
                    for v in range(2):
                        col = (4 * d + 2 * v + d) * P + (P - 1) * (1 - d)
                        m = act.activation(Kt[:, d, v, :], qkn[:, 2 + d, :], IDT, scale=eD[:, col:col + 1])
                m.then_inc(ktail_ready, 1)
                nxt(3)
                for d in range(2):
                    act.wait_ge(t0_ps, h * 2 + (d + 1))
                    act.activation(Tm[:, 4 * d:4 * d + 4, :].rearrange("p u i -> p (u i)"), ps[:, TT[d], :],
                                   IDT).then_inc(t0_ready, 1)
                for l in range(LV):
                    for d in range(2):
                        act.wait_ge(tt_ps, at_level(h, l, d))
                        act.activation(Sm[:, 4 * d:4 * d + 4, :].rearrange("p u i -> p (u i)"), ps[:, TT[d], :],
                                       IDT).then_inc(s_ready, 1)
                    if l == 0:
                        nxt(4)
                    if l == 2:
                        nxt(5)
                for d in range(2):
                    act.wait_ge(u0_ps, h * 2 + (d + 1))
                    act.activation(Vn[:, 4 * d:4 * d + 4, :].rearrange("p (v c) i -> p v c i", v=2)[:, :, d, :],
                                   ps[:, XY[d], 0:256].rearrange("p (v i) -> p v i", v=2), IDT).then_inc(u0_ready, 1)
                for d in range(2):
                    act.wait_ge(ks_ps, h * 4 + (2 * d + 2))
                    for v in range(2):
                        u = 4 * d + 2 * v + 1 - d
                        m = act.activation(QSs[:, 2 * v + 1 - d, :], ps[:, TT[d], 256 + v * P:256 + (v + 1) * P], IDT,
                                           scale=cols[:, 3, u:u + 1])
                    m.then_inc(qs_ready, 1)
                for d in range(2):
                    act.wait_ge(v1_ps, h * 2 + (d + 1))
                    act.activation(Vn[:, 4 * d:4 * d + 4, :].rearrange("p (v c) i -> p v c i", v=2)[:, :, 1 - d, :],
                                   ps[:, XY[d], 0:256].rearrange("p (v i) -> p v i", v=2), IDT).then_inc(v1_ready, 1)
                act.wait_ge(o_ready, h + 1)
                act.wait_ge(ss_ready, h + 1)
                for u in range(4):
                    m = act.activation(junk[:, u * P:(u + 1) * P], Osb[:, u, :], ACT.Square, accum_out=small[:, 48 + u:49 + u])
                m.then_inc(oss_ready, 1)
                act.wait_ge(oT_ps, h + 1)
                act.activation(oT[:, ds(h * 2, 2), :], ps[:, TT[0], :].rearrange("p (v t) -> p v t", v=2), IDT,
                               scale=misc[:, 32:33]).then_inc(oT_ready, 1)

            act.sem_inc(fm_done, 2)
            act.wait_ge(params_ready, 1)
            ch.link(act.activation(cond, misc[:, 0:KT], ACT.Tanh, scale=0.5))
            act.wait_ge(mod_ready, 1)
            pre_norm(0)
            split_hi(act, n_ab, 1, 0, m_ab, 1, 0, 0)
            act.wait_ge(ab_dve, 1)
            act.activation(abw[:, 2, :], abw[:, 1, :], ACT.Tanh, scale=0.5)
            ch.link(act.activation(abw[:, 3, :], abw[:, 0, :], ACT.Abs))
            act.activation(small[:, 2:3], small[:, 0:1], ACT.Exp)
            act.activation(abw[:, 3, :], abw[:, 3, :], ACT.Exp, scale=-1.0).then_inc(ab_act, 1)
            act.wait_ge(ab_dve, 2)
            act.activation(abw[:, 5, :], abw[:, 4, :], ACT.Ln).then_inc(ab_act, 1)
            act.wait_ge(tbl_ready, 1)
            act.activation(tbl[:, 3, :, :], tbl[:, 0, :, :], ACT.Exp).then_inc(ab_act, 1)
            for j in range(6):
                head_hi(0, j)
            act.wait_ge(rows_stored, 64)
            with act.Fori(0, KH - 1) as h:
                core(h, lambda j: head_hi(h + 1, j))
            core(KH - 1, lambda j: None)
            stream(n_dout, m_dout, VH, LOOPM, oT)
            post(0)
            pre_norm(1)
            gateup(n_gu0, m_gu0, 0, LOOPM, 3)
            act.wait_ge(hid_ready, 2 + FT // 2)
            stream(n_dn0, m_dn0, FT, LOOPM, hid)
            post(1)
            pre_norm(2)

            def square(n0, m0, q0, evacuate):
                with act.Fori(0, 4) as i:
                    for r in range(2):
                        for j in range(2):
                            split_hi(act, n0, 4, 2 * r + j, m0, 4, 2 * r + j, i)
                        act.wait_ge(w_used, i * 4 + (m0 + 2 * r + 2))
                        evacuate(i, r)

            act.wait_ge(x_stored, 32)
            square(n_sin, m_sin, 0, lambda i, r: act.activation(
                uT[:, ds(i * 4 + 2 * r, 2), :], ps[:, r, :].rearrange("p (b t) -> p b t", b=2), IDT).then_inc(fm_done, 1))

            act.wait_ge(s5_dve_a, 1)
            act.activation(s5w[:, 5, :], s5w[:, 3, :], ACT.Tanh, scale=0.5).then_inc(s5_act_a, 1)
            act.wait_ge(s5_dve_a, 2)
            act.activation(s5w[:, 9, :], s5w[:, 8, :], ACT.Sin, scale=TWO_PI)
            act.activation(s5w[:, 10, :], s5w[:, 8, :], ACT.Sin, scale=TWO_PI / 2).then_inc(s5_act_a, 1)
            with act.Fori(0, NJ) as j:
                act.wait_ge(bcT_ps, j + 1)
                act.wait_ge(bu_ps, j * 8)
                act.activation(bT.rearrange("p n i -> p (n i)"), ps[:, 0, :], IDT).then_inc(bT_ready, 1)
                for q in range(8):
                    v = j * 8 + q
                    act.wait_ge(ang_ready, j * 8 + (q + 1))
                    if q >= 1:
                        act.wait_ge(psin_ready, j * 8 + (q - 1))
                        act.wait_ge(pcos_ready, j * 8 + (q - 1))
                    else:
                        act.wait_ge(psin_ready, j * 8)
                        act.wait_ge(pcos_ready, j * 8)
                    t = trig[:, q % 2]
                    ch2 = act.activation(angabs[:, q % 2, :], ang[:, q % 2, :], ACT.Abs)
                    ch2.then_inc(abs_done, 1)
                    act.activation(t[:, 1, :], ang[:, q % 2, :], ACT.Sin, scale=TWO_PI)
                    act.activation(t[:, 2, :], ang[:, q % 2, :], ACT.Sin, scale=-TWO_PI)
                    act.wait_ge(abs_done, j * 8 + (q + 1))
                    act.activation(t[:, 0, :], angabs[:, q % 2, :], ACT.Sin, scale=-TWO_PI, bias=small[:, 60:61]).then_inc(trig_ready, 1)
            act.wait_ge(ysum_ready, NJ)
            for half in range(2):
                act.activation(ysb[:, 8 * half:8 * half + 8, :], ysb[:, 8 * half:8 * half + 8, :], ACT.Gelu).then_inc(gelu_done, 1)
            for half in range(2):
                act.wait_ge(gelu_done, half + 1)
                act.activation(hhi[:, 8 * half:8 * half + 8, :], ysb[:, 8 * half:8 * half + 8, :], IDT).then_inc(h_hi, 1)

            def glu_out(i, r):
                act.activation(fth[:, r, :], ps[:, r, :], ACT.Tanh, scale=0.5).then_inc(glu_tanh, 1)

            square(n_glu, m_glu, 8, glu_out)
            act.wait_ge(fm_done, 2 + 16)
            stream(n_sout, m_sout, KT, 0, ysb)
            post(2)
            pre_norm(3)
            gateup(n_gu1, m_gu1, FT // 2, 0, FT // 4)
            act.wait_ge(hid_ready, 2 + FT)
            stream(n_dn1, m_dn1, FT, 0, hid)
            post(3)

        @block.vector
        def _(dve):
            ch = Chain(dve, dves)
            link = ch.link
            tt, ts, stt = dve.tensor_tensor, dve.tensor_scalar, dve.scalar_tensor_tensor

            def finish_mod(f):
                layer, chunks, _ = FINALS[f]
                dve.wait_ge(mod_ps, f + 1)
                lo, n = chunks[0] * KT, len(chunks) * KT
                m = tt(modc[:, layer, lo:lo + n], ps[:, 7, 0:n], modb[:, layer, lo:lo + n], ALU.add)
                m.then_inc(mod_ready, 1)
                dve.wait_ge(mod_ready, f + 1)

            def gate_rows(s):
                layer, sub = SUB[s]["layer"], SUB[s]
                link(tt(gwcol, mod_cols(layer, sub["gt"]), norm_col(sub["post"], layer), ALU.mult))
                for g in range(4):
                    tt(diag[:, g, :, :], rep(ident, 4), bc(gwcol[:, 4 * g:4 * g + 4], P), ALU.mult).then_inc(diag_ready, 1)
                for g in range(4):
                    dve.wait_ge(gw_ps, 4 * s + g + 1)
                    dve.tensor_copy(gwrow_of[s][:, 512 * g:512 * (g + 1)], ps[:, g, :]).then_inc(gw_ready, 1)

            def post(s, eps):
                dve.wait_ge(ss_out, s + 1)
                link(dve.tensor_reduce(small[:, 16:18], small[:, 8:16].rearrange("p (c n) -> p c n", c=2), AX_X, ALU.add))
                link(ts(small[:, 16:18], small[:, 16:18], 1.0 / D, eps, ALU.mult, ALU.add))
                newton(ch, dve, small[:, 18:20], small[:, 16:18], small[:, 20:22])
                dve.wait_ge(gw_ready, 4 * s + 4)
                for c in range(NT):
                    for n in range(4):
                        m = stt(out=ptmp[:, c, 512 * n:512 * (n + 1)], in0=ps[:, 4 * c + n, :],
                                scalar=small[:, 18 + c:19 + c], in1=gwrow_of[s][:, 512 * n:512 * (n + 1)],
                                op0=ALU.mult, op1=ALU.mult)
                link(m)
                dve.wait_ge(x_landed, 16 * (s + 2))
                tt(xbuf, xbuf, ptmp, ALU.add).then_inc(x_new, 1)

            def pre_norm(s):
                layer, sub = SUB[s]["layer"], SUB[s]
                stt(out=acol, in0=mod_cols(layer, sub["sc"]), scalar=1.0, in1=norm_col(sub["pre"], layer),
                    op0=ALU.add, op1=ALU.mult)
                dve.wait_ge(ss_x, s + 1)
                link(ts(small[:, 26:28], small[:, 24:26], 1.0 / D, EPS, ALU.mult, ALU.add))
                newton(ch, dve, small[:, 28:30], small[:, 26:28], small[:, 30:32])
                dve.sem_inc(rstd_x, 1)
                for k in range(KT):
                    t = htmp[:, k % 2, :]
                    dve.wait_ge(h_hi, H_HI[s] + 2 * (k // 2) + 2)
                    link(ts(t, ps[:, k // 2, (k % 2) * T:(k % 2 + 1) * T], acol[:, k:k + 1],
                            mod_cols(layer, sub["sh"])[:, k:k + 1], ALU.mult, ALU.add))
                    m = tt(hlo[:, k, :], t, hhi[:, k, :].bitcast(F32), ALU.subtract)
                m.then_inc(h_ready, 1)

            def stream(n0, m0, kts, lm, src, acc, mods):
                for nb, mb, kb_, trips, per, first, last in plan(n0, m0, kts, lm):
                    def body(i):
                        for j in range(4):
                            stage_lo(dve, src[:, ds(i * 4 + (kb_ + j), 1), :].rearrange("p o t -> p (o t)"),
                                     mb, 4, j, i)
                            split_lo(dve, nb, per, raw_at(per, j), mb, 4, j, i)
                            if per == 8 and j % 2 == 1:
                                r = j // 2
                                for c in range(2):
                                    mod_acc(dve, nb, i, 8, 4 * r + 2 + c, acc[:, c, :], i * 2 + (kb_ // 2 + r))
                    run(dve, trips, body)

            def gate_up_out(q, r, jq, m_done):
                dve.wait_ge(gate_tanh, q + 1)
                stt(out=ftt[:, r, :], in0=fth[:, r, :], scalar=1.0, in1=ps[:, r, :], op0=ALU.add,
                    op1=ALU.mult).then_inc(gate_used, 1)
                dve.wait_ge(gate_used, q + 3)
                dve.wait_ge(w_used, m_done)
                tt(hid[:, ds(jq * 2, 2), :], ftt[:, r, :].rearrange("p (b t) -> p b t", b=2),
                   ps[:, 2 + r, :].rearrange("p (b t) -> p b t", b=2), ALU.mult).then_inc(hid_ready, 1)

            def gateup(n0, m0, q0, lm, lp):
                def tiles(i, nb, nper, mb, r):
                    jn = (nper // 2) * r
                    for j in range(4):
                        split_lo(dve, nb, nper, jn + j, mb, 8, 4 * r + j, i)
                    if nper == 16:
                        for c in range(4):
                            mod_acc(dve, nb, i, 16, jn + 4 + c, macc4[:, c, :], i * 2 + r)
                def pairs(i, nb, nper, mb, q):
                    for r in range(2):
                        tiles(i, nb, nper, mb, r)
                        gate_up_out(i * 2 + (q + r), r, i * 2 + (q - q0 + r), i * 8 + (mb + 4 * r + 4))
                if lm:
                    with dve.Fori(0, lm) as i:
                        pairs(i, n0, 16, m0, q0)
                with dve.Fori(0, lp) as i:
                    pairs(i, n0 + 16 * lm, 8, m0 + 8 * lm, q0 + 2 * lm)

            def head_lo(h, j):
                split_lo(dve, n_head, PER_HEAD, j, m_head, 6, j, h)

            def head_mod(h, j):
                mod_acc(dve, n_head, h, PER_HEAD, 6 + j, macc[:, j, :], h)

            CHAIN_PER_HEAD = HEAD_LINKS

            def load_convw(h):
                for t, first in ((0, 0), (1, KH)):
                    dve.tensor_copy(convh[:, t, :], convw[:, :, ds(h + first, 1)].rearrange("p j o -> p (j o)"))
                link(dve.tensor_copy(convh[:, 2:4, :].rearrange("p t j -> p j t"), convw[:, :, ds(h * 2 + 2 * KH, 2)]))

            def core(h, nxt, mod):
                load_convw(h)
                dve.tensor_copy(cols, tbl[:, :, ds(h, 1), :].rearrange("p k o u -> p k (o u)"))
                nxt(0)
                for t in range(4):
                    if t % 2 == 0:
                        dve.wait_ge(cbuf_ready, h * 2 + (t // 2 + 1))
                    y = yact[:, t * T:(t + 1) * T]
                    link(ts(y, cbuf[:, t, 0:T], convh[:, t, 0:1], None, ALU.mult))
                    for j in range(1, CK):
                        m = stt(out=y, in0=cbuf[:, t, j:j + T], scalar=convh[:, t, j:j + 1], in1=y,
                                op0=ALU.mult, op1=ALU.add)
                        if j < CK - 1:
                            link(m)
                m.then_inc(conv_done, 1)
                nxt(1)
                dve.wait_ge(silu_tanh, h + 1)
                dve.wait_ge(conv_done, h + 1)
                stt(out=yact, in0=eD, scalar=1.0, in1=yact, op0=ALU.add, op1=ALU.mult).then_inc(act_done, 1)
                dve.wait_ge(z_tanh, h + 1)
                zview = lambda v: v.rearrange("p (c v i) -> p v c i", c=2, v=2)
                for v in range(2):
                    m = stt(out=zg[:, 2 * v:2 * v + 2, :], in0=zth.rearrange("p (c v) i -> p v c i", v=2)[:, v],
                            scalar=1.0, in1=zview(ps[:, Z_BANK, :])[:, v], op0=ALU.add, op1=ALU.mult)
                m.then_inc(zg_ready, 1)
                nxt(2)
                dve.wait_ge(rows_landed, h * 64 + 64)
                dve.wait_ge(act_done, h + 1)
                for u in range(8):
                    m = ts(eD[:, u * P:(u + 1) * P], grow[:, u, :], cols[:, 0, u:u + 1], 0.0, ALU.subtract, ALU.min)
                m.then_inc(de_ready, 1)
                dve.wait_ge(ss_ready, h + 1)
                link(ts(small[:, 36:40], small[:, 32:36], 4.0 * EPS, None, ALU.add))
                newton(ch, dve, small[:, 40:44], small[:, 36:40], small[:, 44:48])
                tt(qkn, ps[:, TT[0], :].rearrange("p (u i) -> p u i", u=4), bc(small[:, 40:44], P),
                   ALU.mult).then_inc(qkn_ready, 1)
                for d in range(2):
                    m = tt(Vb[:, 4 * d:4 * d + 4, :], ps[:, TT[1], :].rearrange("p (u i) -> p u i", u=4),
                           bc(cols[:, 1, 4 * d:4 * d + 4], P), ALU.mult)
                m.then_inc(vb_ready, 1)
                dve.wait_ge(kk_ps, h + 1)
                for d in range(2):
                    for m_ in range(2):
                        m = tt(km[:, d, m_, :, :], ps[:, K_BANK, m_ * 256:(m_ + 1) * 256].rearrange("p (c i) -> p c i", c=2),
                               rep(mkq[:, d, m_, :], 2), ALU.mult)
                m.then_inc(km_ready, 1)
                nxt(3)
                dve.wait_ge(km_ready, h + 1)
                for d in range(2):
                    dve.wait_ge(eb_ready, h * 2 + (d + 1))
                    for v in range(2):
                        u = 4 * d + 2 * v
                        m = tt(Bm[:, u:u + 2, :], Bm[:, u:u + 2, :], km[:, d, 0, :, :], ALU.mult)
                    link(m)
                    link(tt(Sm[:, 4 * d:4 * d + 4, :], Bm[:, 4 * d:4 * d + 4, :], rep(m1[:, d, :], 4), ALU.mult))
                    tt(Sm[:, 4 * d:4 * d + 4, :], Sm[:, 4 * d:4 * d + 4, :], rep(ident, 4), ALU.add).then_inc(s0_ready, 1)
                for l in range(LV):
                    for d in range(2):
                        dve.wait_ge(x_ps, at_level(h, l, d))
                        tt(Xm[:, d, :, :], ps[:, XY[d], 0:256].rearrange("p (u n) -> p u n", u=4),
                           rep(mlv[:, l, d, :], 4), ALU.mult).then_inc(xm_ready, 1)
                    for d in range(2):
                        dve.wait_ge(y_ps, at_level(h, l, d))
                        t = changed(Tm[:, 4 * d:4 * d + 4, :], l, d)
                        tt(t, t, ps[:, XY[d], 256:512].rearrange("p (u n b) -> p u n b", u=4, b=2 << l),
                           ALU.add).then_inc(t_ready, 1)
                    if l == 0:
                        nxt(4)
                    if l == 2:
                        nxt(5)
                    if l == 4:
                        mod(0)
                for d in range(2):
                    dve.wait_ge(st_ps, h * 2 + (d + 1))
                    dve.tensor_copy(Ssb[:, d, :, :].rearrange("p v i -> p (v i)"), ps[:, TT[d], 0:256]).then_inc(st_ready, 1)
                for d in range(2):
                    dve.wait_ge(ks_ps, h * 4 + (2 * d + 1))
                    for v in range(2):
                        u = 4 * d + 2 * v + 1 - d
                        m = stt(out=R1[:, d, v, :], in0=ps[:, XY[d], 256 + v * P:256 + (v + 1) * P],
                                scalar=cols[:, 2, u:u + 1], in1=Vb[:, u, :], op0=ALU.mult, op1=ALU.add)
                    m.then_inc(r1_ready, 1)
                mod(1)
                dve.wait_ge(o_ps, h + 1)
                dve.wait_ge(qs_ready, h * 2 + 2)
                tt(Osb, ps[:, K_BANK, :].rearrange("p (u i) -> p u i", u=4), QSs, ALU.add).then_inc(o_ready, 1)
                dve.wait_ge(oss_ready, h + 1)
                link(ts(small[:, 52:56], small[:, 48:52], 1.0 / P, EPS, ALU.mult, ALU.add))
                newton(ch, dve, small[:, 56:60], small[:, 52:56], small[:, 44:48])
                dve.wait_ge(o_ready, h + 1)
                link(tt(Osb, Osb, bc(small[:, 56:60], P), ALU.mult))
                tt(Osb, Osb, zg, ALU.mult).then_inc(og_ready, 1)

            dve.sem_inc(gate_used, 2)
            dve.sem_inc(hid_ready, 2)
            dve.wait_ge(params_T, 1)
            dve.tensor_copy(normc, ps[:, 0, 0:P])
            dve.tensor_copy(modb[:, 0, :], ps[:, 0, P:P + 96])
            dve.tensor_copy(modb[:, 1, :], ps[:, 0, 2 * P:2 * P + 96])
            link(dve.tensor_copy(misc, ps[:, 0, 3 * P:3 * P + 33]))
            cw = convw.rearrange("p j t -> p (j t)")
            dve.tensor_copy(cw[:, 0:P], ps[:, 1, 0:P])
            dve.tensor_copy(cw[:, P:2 * P], ps[:, 1, P:2 * P])
            dve.tensor_copy(cw[:, 2 * P:320], ps[:, 1, 2 * P:2 * P + 64])
            dve.tensor_scalar(small[:, 60:61], ones[:, 0:1], math.pi / 2, None, ALU.mult)
            ts(misc[:, 32:33], misc[:, 32:33], 0.5, None, ALU.mult).then_inc(params_ready, 1)
            dve.wait_ge(acts, 1)
            link(stt(out=cond, in0=cond, scalar=1.0, in1=misc[:, 0:KT], op0=ALU.add, op1=ALU.mult))
            link(ts(cond, cond, 0.5, None, ALU.mult))
            dve.wait_ge(macc_zero, 1)
            for j in range(2):
                mod_acc(dve, 0, 0, 2, j, macc[:, j, :], 0)
            with dve.Fori(0, KT - 1) as k:
                for j in range(2):
                    mod_acc(dve, 2, k, 2, j, macc[:, j, :], k + 1)
            finish_mod(0)
            pre_norm(0)
            split_lo(dve, n_ab, 1, 0, m_ab, 1, 0, 0)

            dve.wait_ge(w_used, 1)
            ts(abw[:, 0, :], ps[:, 4, 0:T], small[:, 1:2], None, ALU.add)
            dve.tensor_copy(abw[:, 1, :], ps[:, 4, 0:T]).then_inc(ab_dve, 1)
            dve.wait_ge(ab_act, 1)
            ts(abw[:, 2, :], abw[:, 2, :], 0.5, 0.5, ALU.mult, ALU.add)
            ts(abw[:, 4, :], abw[:, 3, :], 1.0, None, ALU.add).then_inc(ab_dve, 1)
            dve.wait_ge(ab_dve, 2)
            link(dve.reciprocal(abw[:, 6, :], abw[:, 4, :]))
            link(ts(abw[:, 7, :], abw[:, 4, :], -1.0, None, ALU.add))
            link(tt(abw[:, 7, :], abw[:, 3, :], abw[:, 7, :], ALU.subtract))
            link(tt(abw[:, 7, :], abw[:, 7, :], abw[:, 6, :], ALU.mult))
            dve.wait_ge(ab_act, 2)
            link(tt(abw[:, 5, :], abw[:, 5, :], abw[:, 7, :], ALU.add))
            link(stt(out=abw[:, 0, :], in0=abw[:, 0, :], scalar=0.0, in1=abw[:, 5, :], op0=ALU.max, op1=ALU.add))
            link(ts(abw[:, 0, :], abw[:, 0, :], small[:, 2:3], -1.0, ALU.mult, ALU.mult))
            for d in range(2):
                r0 = 64 * d
                for c in range(NT):
                    lo, hi = c * P, (c + 1) * P
                    src = abw[r0:r0 + 64, 0, lo:hi]
                    dst = abw[r0:r0 + 64, 1, lo:hi]
                    if d == 1:
                        src, dst = src[:, ::-1], dst[:, ::-1]
                    m = dve.tensor_tensor_scan(dst, ones[r0:r0 + 64, 0:1].to_broadcast([64, P]), src, 0.0,
                                               ALU.mult, ALU.add)
            m.then_inc(ab_dve, 1)
            dve.wait_ge(gT_ps, 1)
            for d in range(2):
                for c in range(NT):
                    out4 = lambda kind: tbl[:, kind, :, :].rearrange("p h (d v c) -> p d c h v", d=2, v=2)[:, d, c]
                    for n, kind, r0 in ((c, 0, 64 * d + 32), (2 + c, 2, 64 * d)):
                        m = dve.tensor_copy(out4(kind), ps[:, 5, n * P + r0:n * P + r0 + 32].rearrange("p (h v) -> p h v", v=2))
            link(m)
            link(ts(tbl[:, 1, :, :], tbl[:, 2, :, :], 0.5, None, ALU.mult))
            dve.sem_inc(tbl_ready, 1)
            dve.wait_ge(ab_act, 3)
            link(stt(out=tbl[:, 2, :, :], in0=tbl[:, 2, :, :], scalar=-1.0, in1=tbl[:, 3, :, :], op0=ALU.mult, op1=ALU.mult))
            link(ts(tbl[:, 3, :, :], tbl[:, 3, :, :], DK_SCALE, None, ALU.mult))

            dve.wait_ge(macc_zero, 2)
            for j in range(6):
                head_lo(0, j)
            for j in range(2):
                head_mod(0, j)
            with dve.Fori(0, KH - 1) as h:
                ch.enter(h, CHAIN_PER_HEAD)
                core(h, lambda j: head_lo(h + 1, j), lambda j: head_mod(h + 1, j))
                ch.leave(CHAIN_PER_HEAD, KH - 1)
            core(KH - 1, lambda j: None, lambda j: None)
            finish_mod(1)
            gate_rows(0)
            dve.wait_ge(macc_zero, 3)
            stream(n_dout, m_dout, VH, LOOPM, oT, macc, True)
            post(0, EPS)
            finish_mod(2)
            pre_norm(1)
            gate_rows(1)
            dve.wait_ge(macc_zero, 4)
            gateup(n_gu0, m_gu0, 0, LOOPM, 3)
            finish_mod(3)
            dve.wait_ge(macc_zero, 5)
            stream(n_dn0, m_dn0, FT, LOOPM, hid, macc4, True)
            post(1, 4.0 * EPS)
            finish_mod(4)
            pre_norm(2)

            def square(n0, m0, evacuate):
                with dve.Fori(0, 4) as i:
                    for r in range(2):
                        for j in range(2):
                            split_lo(dve, n0, 4, 2 * r + j, m0, 4, 2 * r + j, i)
                        evacuate(i, r)

            square(n_sin, m_sin, lambda i, r: None)

            W = lambda n: s5w[:, n, :]
            dve.wait_ge(s5_in, 16 * 11)
            x2, k2, r2, p2, q2 = (s5w[:, 2, n:n + 2] for n in (0, 2, 4, 6, 8))
            link(ts(x2, x2, -87.3, 88.7, ALU.max, ALU.min))
            link(ts(k2, x2, 1.0 / math.log(2.0), ROUND, ALU.mult, ALU.add))
            link(ts(k2, k2, -ROUND, None, ALU.add))
            link(stt(out=r2, in0=k2, scalar=-0.693359375, in1=x2, op0=ALU.mult, op1=ALU.add))
            link(stt(out=r2, in0=k2, scalar=2.12194440e-4, in1=r2, op0=ALU.mult, op1=ALU.add))
            link(ts(p2, r2, 1.0 / 5040.0, None, ALU.mult))
            for f in (720.0, 120.0, 24.0, 6.0, 2.0, 1.0):
                link(stt(out=p2, in0=p2, scalar=1.0 / f, in1=r2, op0=ALU.add, op1=ALU.mult))
            link(ts(p2, p2, 1.0, None, ALU.add))
            link(ts(q2.bitcast(I32), k2, 127.0, 8388608.0, ALU.add, ALU.mult))
            link(tt(p2, p2, q2, ALU.mult))
            step = p2.unsqueeze(2).to_broadcast([P, 2, 64])
            e2 = lambda n: W(n).rearrange("p (e s) -> p e s", e=2)
            link(tt(e2(3), e2(0), step, ALU.mult))
            dve.sem_inc(s5_dve_a, 1)
            link(tt(e2(4), e2(1), step, ALU.mult))
            link(ts(W(6), W(4), 1.0 / (2 * math.pi), ROUND, ALU.mult, ALU.add))
            link(ts(W(6), W(6), -ROUND, None, ALU.add))
            link(stt(out=W(7), in0=W(6), scalar=-6.28125, in1=W(4), op0=ALU.mult, op1=ALU.add))
            link(stt(out=W(7), in0=W(6), scalar=-(2 * math.pi - 6.28125), in1=W(7), op0=ALU.mult, op1=ALU.add))
            link(ts(W(8), W(7), 1.0 / (2 * math.pi), 0.5, ALU.mult, ALU.min))
            link(ts(W(8), W(8), -0.5, None, ALU.max))
            dve.sem_inc(s5_dve_a, 1)
            dve.wait_ge(s5_act_a, 1)
            link(ts(W(11), W(5), -1.0, 1.0, ALU.mult, ALU.add))
            link(dve.reciprocal(W(12), W(11)))
            link(stt(out=W(13), in0=W(5), scalar=2.0, in1=W(12), op0=ALU.mult, op1=ALU.mult))
            link(stt(out=W(14), in0=W(5), scalar=1.0, in1=W(12), op0=ALU.add, op1=ALU.mult))
            dve.wait_ge(s5_act_a, 2)
            link(tt(W(15), W(10), W(10), ALU.mult))
            link(tt(W(15), W(15), W(14), ALU.mult))
            link(stt(out=W(15), in0=W(15), scalar=-2.0, in1=W(13), op0=ALU.mult, op1=ALU.add))
            link(tt(W(16), W(14), W(9), ALU.mult))
            link(tt(W(17), W(0), W(0), ALU.mult))
            link(tt(W(18), W(1), W(1), ALU.mult))
            link(tt(W(17), W(17), W(18), ALU.add))
            link(dve.reciprocal(W(18), W(17)))
            link(tt(W(19), W(15), W(0), ALU.mult))
            link(tt(W(20), W(16), W(1), ALU.mult))
            link(tt(W(19), W(19), W(20), ALU.add))
            link(tt(W(19), W(19), W(18), ALU.mult))
            link(tt(W(21), W(16), W(0), ALU.mult))
            link(tt(W(22), W(15), W(1), ALU.mult))
            link(tt(W(21), W(21), W(22), ALU.subtract))
            link(tt(W(21), W(21), W(18), ALU.mult))
            dve.sem_inc(s5_dve, 1)
            dve.wait_ge(s5_psT, 1)
            for n in range(4):
                link(dve.tensor_copy(s5p[:, n, :], ps[:, 2, n * P:(n + 1) * P]))
            link(ts(s5p[:, 1, GP:2 * GP], s5p[:, 1, GP:2 * GP], -1.0, None, ALU.mult))
            fac = [s5p[:, 2 + r, :].unsqueeze(2).to_broadcast([P, P, Q]) for r in range(2)]
            b3 = [bnat[:, r, :].rearrange("p (g c) -> p g c", c=Q) for r in range(2)]
            y3 = [ysb[:, 8 * r:8 * r + 8, :].rearrange("p k t -> p (k t)").rearrange("p (g c) -> p g c", c=Q) for r in range(2)]
            link(tt(y3[0], b3[1], fac[1], ALU.mult))
            link(tt(y3[1], b3[0], fac[1], ALU.mult))
            for r in range(2):
                link(tt(b3[r], b3[r], fac[0], ALU.mult))
            link(tt(b3[0], b3[0], y3[0], ALU.subtract))
            link(tt(b3[1], b3[1], y3[1], ALU.add))
            dve.sem_inc(s5_ready, 1)
            dve.wait_ge(s5_act, 1)
            with dve.Fori(0, NJ) as j:
                ch.enter(j, S5_LINKS)
                ph, rr_, dd = colj[:, 0:8], colj[:, 8:16], colj[:, 16:17]
                link(dve.tensor_copy(ph.rearrange("p (d g) -> p d g", d=2),
                                     s5p[:, 1, :].rearrange("p (d g) -> p d g", d=2)[:, :, ds(j * 4, 4)]))
                dve.tensor_copy(rr_.rearrange("p (d g) -> p d g", d=2),
                                s5p[:, 0, :].rearrange("p (d g) -> p d g", d=2)[:, :, ds(j * 4, 4)])
                link(dve.tensor_copy(dd, misc[:, ds(j + KT, 1)]))
                dve.wait_ge(bcT_ps, j + 1)
                dve.wait_ge(ymm, j * 8)
                for sgn in range(2):
                    m = tt(cj[:, sgn, :].rearrange("p (n i) -> p n i", n=4), ps[:, 1, :].rearrange("p (n i) -> p n i", n=4),
                           rep(gmask[:, sgn, :], 4), ALU.mult)
                m.then_inc(cj_ready, 1)

                def angle(q):
                    g, d = q // 2, q % 2
                    f = ph[:, 4 * d + g:4 * d + g + 1]
                    link(ts(kb, iota, f, ROUND, ALU.mult, ALU.add))
                    link(ts(kc, kb, -ROUND, None, ALU.add))
                    if q >= 1:
                        dve.wait_ge(trig_ready, j * 8 + (q - 1))
                    else:
                        dve.wait_ge(trig_ready, j * 8)
                    stt(out=ang[:, q % 2, :], in0=iota, scalar=f, in1=kc, op0=ALU.mult, op1=ALU.subtract)\
                        .then_inc(ang_ready, 1)

                angle(0)
                for q in range(8):
                    g, d = q // 2, q % 2
                    if q < 7:
                        angle(q + 1)
                    tr = trig[:, q % 2]
                    bu = ps[:, 2 + q % 2, :].rearrange("p (n t) -> p n t", n=2)
                    dve.wait_ge(trig_ready, j * 8 + (q + 1))
                    dve.wait_ge(bu_ps, j * 8 + (q + 1))
                    dve.wait_ge(zin_ready, j * 8 + q)
                    tt(tc_, rep(tr[:, 0, :], 2), bu, ALU.mult)
                    tt(ts_, tr[:, 1:3, :], bu[:, ::-1, :], ALU.mult).then_inc(t_prod, 1)
                    dve.wait_ge(zin_ready, j * 8 + (q + 1))
                    dve.wait_ge(psin_ready, j * 8 + q)
                    r = rr_[:, 4 * d + g:4 * d + g + 1].to_broadcast([P, T])
                    for n in range(2):
                        o, i_ = zst[:, n, :], zin[:, n, :]
                        if d == 1:
                            o, i_ = o[:, ::-1], i_[:, ::-1]
                        m = dve.tensor_tensor_scan(o, r, i_, 0.0, ALU.mult, ALU.add)
                    m.then_inc(z_ready, 1)
                    dve.wait_ge(z_ready, j * 8 + (q + 1))
                    dve.wait_ge(ymm, j * 8 + q)
                    tt(pcos, rep(tr[:, 0, :], 2), zst, ALU.mult).then_inc(pcos_ready, 1)
                dve.wait_ge(ymm, j * 8 + 8)
                stt(out=ysb[:, ds(j, 1), :].rearrange("p o t -> p (o t)"), in0=uj, scalar=dd,
                    in1=ps[:, 4, 0:T], op0=ALU.mult, op1=ALU.add).then_inc(ysum_ready, 1)
                ch.leave(S5_LINKS, NJ)
            gate_rows(2)
            for half in range(2):
                dve.wait_ge(h_hi, H_HI[3] - 2 + half + 1)
                s_ = slice(8 * half, 8 * half + 8)
                tt(hlo[:, s_, :], ysb[:, s_, :], hhi[:, s_, :].bitcast(F32), ALU.subtract).then_inc(glu_h, 1)

            def glu_out(i, r):
                dve.wait_ge(glu_tanh, i * 2 + (r + 1))
                y = ysb[:, ds(i * 4 + 2 * r, 2), :]
                stt(out=y.rearrange("p b t -> p (b t)"), in0=fth[:, r, :], scalar=1.0,
                    in1=y.rearrange("p b t -> p (b t)"), op0=ALU.add, op1=ALU.mult).then_inc(fm_done, 1)

            dve.wait_ge(gelu_done, 2)
            square(n_glu, m_glu, glu_out)
            stream(n_sout, m_sout, KT, 0, ysb, None, False)
            post(2, 4.0 * EPS)
            pre_norm(3)
            gate_rows(3)
            gateup(n_gu1, m_gu1, FT // 2, 0, FT // 4)
            stream(n_dn1, m_dn1, FT, 0, hid, None, False)
            post(3, 4.0 * EPS)


_INS = ["x", "c", "mod_w", "mod_b", "norm_pre_mix", "norm_post_mix", "norm_pre_ffn", "norm_post_ffn", "dn_w_in",
        "dn_conv_w", "dn_a_log", "dn_dt_bias", "dn_norm_w", "dn_w_out", "s5_w_in", "s5_lam_re", "s5_lam_im",
        "s5_log_step", "s5_b_re", "s5_b_im", "s5_c_re", "s5_c_im", "s5_d", "s5_w_glu", "s5_w_out", "ffn_w_gate",
        "ffn_w_up", "ffn_w_down"]


def kernel(**inputs):
    import numpy as np
    import concourse.bacc as bacc
    from concourse.bass_utils import run_bass_kernel_spmd

    nc = bacc.Bacc("TRN2", target_bir_lowering=False, num_devices=1)
    arrays, aps = {}, {}
    for name in _INS:
        arrays[f"in_{name}"] = np.ascontiguousarray(inputs[name])
        aps[name] = nc.dram_tensor(f"in_{name}", arrays[f"in_{name}"].shape, F32, kind="ExternalInput").ap()
    out = nc.dram_tensor("out", arrays["in_x"].shape, F32, kind="ExternalOutput").ap()
    trunk(nc, aps, out)
    result = run_bass_kernel_spmd(nc, [arrays], core_ids=[0])
    return result.results[0]["out"]
```

```python
import math
from contextlib import ExitStack

import concourse.bass as bass
from concourse import mybir

ALU = mybir.AluOpType
ACT = mybir.ActivationFunctionType
F32 = mybir.dt.float32
F32R = mybir.dt.float32r
I32 = mybir.dt.int32
AX_X = mybir.AxisListType.X
ds = bass.ds

P = 128
ARENA = 27648
RAW = 2
RAW4 = 4
TILE = 2048
ROUND = 12582912.0
RSQRT_SEED = float(0x5F3759DF)
EPS = 1e-6
TWO_PI = 6.2831845
HEAD_LINKS = 44
S5_LINKS = 19
S5OUT = (14, 8, 19, 21)


class Chain:

    def __init__(self, eng, sem):
        self.eng, self.sem, self.n, self.off = eng, sem, 0, 0

    def link(self, ins):
        ins.then_inc(self.sem, 1)
        self.n += 1
        self.eng.wait_ge(self.sem, self.off + self.n)

    def mark(self, ins):
        ins.then_inc(self.sem, 1)
        self.n += 1

    def after(self, back):
        self.eng.wait_ge(self.sem, self.off + (self.n - back))

    def enter(self, i, per):
        self.off, self.start = i * per, self.n

    def leave(self, per, trips):
        assert self.n - self.start == per, (self.n - self.start, per)
        self.n, self.off = self.start + per * trips, 0


def trunk(nc, a, out):
    T, D = a["x"].shape[1], a["x"].shape[2]
    KT = D // P
    NT = T // P
    FT = a["ffn_w_gate"].shape[2] // P
    VH = a["dn_a_log"].shape[2]
    KH = VH // 2
    DV = VH * P
    QOFF, KOFF, VOFF, ZOFF, ABOFF = 0, KH * P, 2 * KH * P, 2 * KH * P + DV, 2 * KH * P + 2 * DV
    CK = a["dn_conv_w"].shape[1]
    PAD = CK // 2
    G, PS, Q = a["s5_b_re"].shape[2:5]
    GP = G // 2
    NJ = G * Q // P
    LV = 6
    DK_SCALE = float(P) ** -0.5
    assert T == 2 * P and D == 2048 and NT == 2 and G * PS == GP * P and Q * 8 == P

    ctx = ExitStack()
    with ctx:
        def sb(name, cols, dt=F32):
            return ctx.enter_context(nc.sbuf_tensor(name, [P, cols], dt))[:, :]

        def sem(name):
            return ctx.enter_context(nc.semaphore(name))

        def dram(name, shape):
            return nc.dram_tensor(name, shape, F32).ap()

        raw = sb("raw", RAW * TILE).rearrange("p (s n) -> p s n", s=RAW)
        whi = sb("whi", 2 * TILE, F32R).rearrange("p (s n) -> p s n", s=2)
        wlo = sb("wlo", 2 * TILE, F32R).rearrange("p (s n) -> p s n", s=2)
        hhi = sb("hhi", KT * T, F32R).rearrange("p (k t) -> p k t", k=KT)
        hlo = sb("hlo", KT * T, F32R).rearrange("p (k t) -> p k t", k=KT)
        shi = sb("shi", 2 * T, F32R).rearrange("p (s t) -> p s t", s=2)
        slo = sb("slo", 2 * T, F32R).rearrange("p (s t) -> p s t", s=2)
        ident = sb("ident", P)
        ones = sb("ones", P)
        normc = sb("normc", 128)
        modb = sb("modb", 192).rearrange("p (l n) -> p l n", l=2)
        modc = sb("modc", 192).rearrange("p (l n) -> p l n", l=2)
        misc = sb("misc", 33)
        cond = sb("cond", KT)
        acol = sb("acol", KT)
        gwcol = sb("gwcol", 4 * KT).rearrange("p (s k) -> p s k", s=4)
        small = sb("small", 64)
        tbl = sb("tbl", 4 * 128).rearrange("p (k h u) -> p k h u", k=4, h=KH)
        cols = sb("cols", 32).rearrange("p (k u) -> p k u", k=4)
        convw = sb("convw", 320).rearrange("p (j t) -> p j t", j=CK)
        convh = sb("convh", 20).rearrange("p (t j) -> p t j", t=4)
        mkq = sb("mkq", 512).rearrange("p (d m i) -> p d m i", d=2, m=2)
        m1 = sb("m1", 256).rearrange("p (d i) -> p d i", d=2)
        mlv = sb("mlv", 2 * LV * 64).rearrange("p (l d n) -> p l d n", l=LV, d=2)
        junk = sb("junk", 512)

        ps = ctx.enter_context(nc.psum_tensor("ps", [P, 8, 512], F32))[:, :, :]

        A = ctx.enter_context(nc.sbuf_tensor("arena", [P, ARENA], F32))[:, :]
        def region(at, n):
            assert at + n <= ARENA, at + n
            return A[:, at:at + n]

        def four(v, n):
            return v.rearrange("p (u i) -> p u i", u=n)

        oT = region(0, 8192).rearrange("p (k t) -> p k t", k=VH)
        macc = region(8192, 4096).rearrange("p (c n) -> p c n", c=2)
        gwrow_mix = region(12288, 2048)
        yact = region(14336, 1024)
        eD = region(15360, 1024)
        qkn = four(region(16384, 512), 4)
        qkT = four(region(16896, 512), 4)
        km = region(17408, 1024).rearrange("p (d m c i) -> p d m c i", d=2, m=2, c=2)
        grow = four(region(18432, 1024), 8)
        brow = four(region(19456, 1024), 8)
        Bm = four(region(20480, 1024), 8)
        Aqk = four(region(21504, 1024), 8)
        Sm = four(region(22528, 1024), 8)
        Tm = four(region(23552, 1024), 8)
        Xm = region(24576, 512).rearrange("p (d u n) -> p d u n", d=2, u=4)
        Vb = four(region(25088, 1024), 8)
        R1 = region(12288, 512).rearrange("p (d v i) -> p d v i", d=2, v=2)
        Kt = region(12800, 512).rearrange("p (d v i) -> p d v i", d=2, v=2)
        Ssb = region(13312, 512).rearrange("p (d v i) -> p d v i", d=2, v=2)
        Vn = four(region(26112, 1024), 8)
        cbuf = region(26112, 1040).rearrange("p (t n) -> p t n", t=4)
        QSs = four(A[:, 18432:18944], 4)
        Osb = four(A[:, 18944:19456], 4)
        zth = four(A[:, 26112:26624], 4)
        zg = four(A[:, 13824:14336], 4)
        abw = region(15360, 2048).rearrange("p (n t) -> p n t", n=8)
        ptmp = region(17408, 4096).rearrange("p (c n) -> p c n", c=2)
        hfull = [region(at, 1024).rearrange("p (k t) -> p k t", k=4)
                 for at in (8192, 9216, 10240, 21504)]
        hid = region(0, 11264).rearrange("p (k t) -> p k t", k=FT)
        gwrow_ffn = region(11264, 2048)
        macc4 = region(13312, 8192).rearrange("p (c n) -> p c n", c=4)
        fth = region(21504, 1024).rearrange("p (s n) -> p s n", s=2)
        ftt = region(22528, 1024).rearrange("p (s n) -> p s n", s=2)
        xbuf = region(0, 4096).rearrange("p (c n) -> p c n", c=2)
        xn = region(4096, 4096).rearrange("p (c n) -> p c n", c=2)
        pin = region(14336, 1024).rearrange("p (n i) -> p n i", n=8)
        uT = region(0, 4096).rearrange("p (k t) -> p k t", k=KT)
        ysb = region(4096, 4096).rearrange("p (k t) -> p k t", k=KT)
        bnat = region(8192, 4096).rearrange("p (r n) -> p r n", r=2)
        cnat = region(12288, 4096).rearrange("p (r d j s) -> p r d j s", r=2, d=2, j=NJ)
        s5p = region(16384, 1024).rearrange("p (n i) -> p n i", n=8)
        gmask = region(17408, 256).rearrange("p (s i) -> p s i", s=2)
        iota = region(17664, 256)
        uj = region(17920, 256)
        cj = region(18176, 1024).rearrange("p (s n) -> p s n", s=2)
        bx = region(19200, 512).rearrange("p (n i) -> p n i", n=4)
        bT = region(19712, 512).rearrange("p (n i) -> p n i", n=4)
        cdup = region(20224, 512).rearrange("p (n i) -> p n i", n=4)
        raws = raw.rearrange("p s n -> p (s n)")
        trig = raws[:, 0:3072].rearrange("p (s n t) -> p s n t", s=4, n=3)
        pcos = raws[:, 3072:4096].rearrange("p (s n t) -> p s n t", s=2, n=2)
        zin = region(20736, 1024).rearrange("p (s n t) -> p s n t", s=2, n=2)
        zst = region(21760, 1024).rearrange("p (s n t) -> p s n t", s=2, n=2)
        ang = region(22784, 512).rearrange("p (s t) -> p s t", s=2)
        kb = region(23296, 256)
        kc = junk[:, 0:256]
        angabs = region(26640, 512).rearrange("p (s t) -> p s t", s=2)
        tprod = region(23552, 2048).rearrange("p (s k n t) -> p s k n t", s=2, k=2, n=2)
        psin = region(25600, 1024).rearrange("p (s n t) -> p s n t", s=2, n=2)
        colj = cols.rearrange("p k u -> p (k u)")
        s5w = region(17920, 4096).rearrange("p (n i) -> p n i", n=32)

        more = region(23552, 2 * TILE).rearrange("p (s n) -> p s n", s=2)
        ring4 = [raw[:, 0, :], raw[:, 1, :], more[:, 0, :], more[:, 1, :]]

        x_dram = [dram(f"x_resid{s}", [T, D]) for s in range(3)]
        g_rows = dram("g_rows", [2 * VH, T])
        b_rows = dram("b_rows", [2 * VH, T])
        gw_rows = dram("gw_rows", [4, D])

        raw_landed = [sem(f"raw_landed{s}") for s in range(RAW)]
        ring_landed = [sem(f"ring_landed{s}") for s in range(RAW4)]
        raw_used = sem("raw_used")
        hi_ready = sem("hi_ready")
        w_used = sem("w_used")
        acts = sem("act_chain")
        dves = sem("dve_chain")
        pools = sem("pool_chain")
        consts_ready = sem("consts_ready")
        params_in = sem("params_in")
        params_T = sem("params_T")
        params_ready = sem("params_ready")
        macc_zero = sem("macc_zero")
        mod_ps = sem("mod_ps")
        mod_ready = sem("mod_ready")
        gw_col = sem("gw_col")
        gw_stored = sem("gw_stored")
        gw_landed = sem("gw_landed")
        x_landed = sem("x_landed")
        x_stored = sem("x_stored")
        ss_out = sem("ss_out")
        x_new = sem("x_new")
        ss_x = sem("ss_x")
        rstd_x = sem("rstd_x")
        xn_ready = sem("xn_ready")
        xnT_ps = sem("xnT_ps")
        h_act = sem("h_act")
        h_dve = sem("h_dve")
        h_hi = sem("h_hi")
        h_ready = sem("h_ready")
        ab_act = sem("ab_act")
        ab_dve = sem("ab_dve")
        gT_ps = sem("gT_ps")
        rows_stored = sem("rows_stored")
        tbl_ready = sem("tbl_ready")
        cbuf_ready = sem("cbuf_ready")
        conv_done = sem("conv_done")
        zg_ready = sem("zg_ready")
        ymm = sem("ymm")
        silu_tanh = sem("silu_tanh")
        act_done = sem("act_done")
        tok_ps = sem("tok_ps")
        ss_ready = sem("ss_ready")
        qkn_ready = sem("qkn_ready")
        vb_ready = sem("vb_ready")
        qkT_ps = sem("qkT_ps")
        qkT_ready = sem("qkT_ready")
        kk_ps = sem("kk_ps")
        km_ready = sem("km_ready")
        rows_landed = sem("rows_landed")
        de_ready = sem("de_ready")
        e_ready = sem("e_ready")
        eb_ready = sem("eb_ready")
        aqk_ready = sem("aqk_ready")
        s0_ready = sem("s0_ready")
        t0_ps = sem("t0_ps")
        t0_ready = sem("t0_ready")
        x_ps = sem("x_ps")
        xm_ready = sem("xm_ready")
        y_ps = sem("y_ps")
        t_ready = sem("t_ready")
        tt_ps = sem("tt_ps")
        s_ready = sem("s_ready")
        ktail_ready = sem("ktail_ready")
        u0_ps = sem("u0_ps")
        u0_ready = sem("u0_ready")
        st_ps = sem("st_ps")
        st_ready = sem("st_ready")
        ks_ps = sem("ks_ps")
        r1_ready = sem("r1_ready")
        qs_ready = sem("qs_ready")
        v1_ps = sem("v1_ps")
        v1_ready = sem("v1_ready")
        o_ps = sem("o_ps")
        o_ready = sem("o_ready")
        oss_ready = sem("oss_ready")
        z_tanh = sem("z_tanh")
        og_ready = sem("og_ready")
        oT_ps = sem("oT_ps")
        oT_ready = sem("oT_ready")
        gate_tanh = sem("gate_tanh")
        gate_used = sem("gate_used")
        hid_ready = sem("hid_ready")
        fm_done = sem("fm_done")
        s5_in = sem("s5_in")
        s5_act = sem("s5_act")
        s5_dve = sem("s5_dve")
        s5_dve_a = sem("s5_dve_a")
        s5_act_a = sem("s5_act_a")
        abs_done = sem("abs_done")
        s5_psT = sem("s5_psT")
        s5_ready = sem("s5_ready")
        bx_ready = sem("bx_ready")
        cdup_ready = sem("cdup_ready")
        bcT_ps = sem("bcT_ps")
        bT_ready = sem("bT_ready")
        cj_ready = sem("cj_ready")
        ang_ready = sem("ang_ready")
        trig_ready = sem("trig_ready")
        bu_ps = sem("bu_ps")
        t_prod = sem("t_prod")
        zin_ready = sem("zin_ready")
        z_ready = sem("z_ready")
        psin_ready = sem("psin_ready")
        pcos_ready = sem("pcos_ready")
        ysum_ready = sem("ysum_ready")
        gelu_done = sem("gelu_done")
        glu_h = sem("glu_h")
        glu_tanh = sem("glu_tanh")

        MODK = a["mod_w"]
        LOOPM = 8
        n_ab = 2 * KT
        n_head = n_ab + 1
        PER_HEAD = 8
        n_dout = n_head + PER_HEAD * KH
        n_gu0 = n_dout + VH + 2 * KT
        n_dn0 = n_gu0 + 2 * 2 * FT // 2 + 4 * KT
        n_sin = n_dn0 + FT + 2 * KT
        n_glu = n_sin + KT
        n_sout = n_glu + KT
        n_gu1 = n_sout + KT
        n_dn1 = n_gu1 + 2 * FT
        m_ab, m_head = 0, 1
        m_dout = m_head + 6 * KH
        m_gu0 = m_dout + VH
        m_dn0 = m_gu0 + 2 * FT
        m_sin = m_dn0 + FT
        m_glu = m_sin + KT
        m_sout = m_glu + KT
        m_gu1 = m_sout + KT
        m_dn1 = m_gu1 + 2 * FT

        post_m = [m_gu0, m_sin, m_gu1, m_dn1 + FT]

        def slot(n0, j):
            return raw[:, (n0 + j) % RAW, :] if n0 < n_dout else ring4[(n0 - n_dout + j) % RAW4]

        def load(sp, n0, i, per, j, src, view=None):
            ring, base, sems = (RAW, 0, raw_landed) if n0 < n_dout else (RAW4, n_dout, ring_landed)
            if n0 + j >= ring:
                sp.wait_ge(raw_used, i * per + (n0 + j - ring + 1))
            dst = slot(n0, j) if view is None else view(slot(n0, j))
            sp.dma_start(dst, src).then_inc(sems[(n0 - base + j) % ring], 16)

        def cols_view(kts):
            return lambda v: v.rearrange("p (k n) -> p k n", k=kts)

        def load_cols(sp, n0, i, per, j, w, k0, kts, c0, width):
            load(sp, n0, i, per, j,
                 w[k0 * P:(k0 + kts) * P, ds(c0, width)].rearrange("(k p) n -> p k n", p=P), view=cols_view(kts))

        def load_rows(sp, n0, i, per, j, w, r0):
            load(sp, n0, i, per, j, w[ds(r0, P), :])

        def load_mod(sp, n0, i, per, j, layer, k, chunk):
            load(sp, n0, i, per, j, MODK[layer, ds(k * P, P), chunk * D:(chunk + 1) * D])

        def landed(eng, n0, i, per, j):
            ring, base, sems = (RAW, 0, raw_landed) if n0 < n_dout else (RAW4, n_dout, ring_landed)
            eng.wait_ge(sems[(n0 - base + j) % ring], i * (per // ring * 16) + 16 * ((n0 - base + j) // ring + 1))

        def split_hi(act, n0, npr, j, m0, mpr, jm, i):
            landed(act, n0, i, npr, j)
            if not isinstance(i, int) or i * mpr + m0 + jm >= 2:
                act.wait_ge(w_used, i * mpr + (m0 + jm - 1))
            act.activation(whi[:, (m0 + jm) % 2, :], slot(n0, j),
                           ACT.Identity).then_inc(hi_ready, 1)

        def split_lo(dve, n0, npr, j, m0, mpr, jm, i):
            dve.wait_ge(hi_ready, i * mpr + (m0 + jm + 1))
            dve.tensor_tensor(wlo[:, (m0 + jm) % 2, :], slot(n0, j),
                              whi[:, (m0 + jm) % 2, :].bitcast(F32), ALU.subtract).then_inc(raw_used, 1)

        def mod_acc(dve, n0, i, per, j, acc, k):
            landed(dve, n0, i, per, j)
            if n0 + j > 0:
                dve.wait_ge(raw_used, i * per + (n0 + j))
            dve.scalar_tensor_tensor(out=acc, in0=slot(n0, j), scalar=cond[:, ds(k, 1)], in1=acc,
                                     op0=ALU.mult, op1=ALU.add).then_inc(raw_used, 1)

        def w_at(mods, j):
            return 2 * j if mods else j

        def split_ready(pe, n0, npr, j, m0, mpr, jm, i):
            pe.wait_ge(raw_used, i * npr + (n0 + j + 1))

        def three(pe, o, lh, ll, rh, rl, start, stop):
            pe.matmul(o, lh, rh, start=start, stop=False, skip_group_check=True)
            pe.matmul(o, lh, rl, start=False, stop=False, skip_group_check=True)
            return pe.matmul(o, ll, rh, start=False, stop=stop, skip_group_check=True)

        def fm_block(pe, o, s, c0, stride, kts, k0, first, last):
            for k in range(kts):
                c = k * stride + c0
                mm = three(pe, o, whi[:, s, c:c + P], wlo[:, s, c:c + P], hhi[:, k0 + k, :], hlo[:, k0 + k, :],
                           first and k == 0, last and k == kts - 1)
            return mm

        def tm_pass(pe, s, st, first, last):
            for c in range(NT):
                h, l = shi[:, st, c * P:(c + 1) * P], slo[:, st, c * P:(c + 1) * P]
                for n in range(4):
                    pe.matmul(ps[:, 4 * c + n, :], h, whi[:, s, n * 512:(n + 1) * 512], start=first, stop=False,
                              skip_group_check=True)
                for n in range(4):
                    pe.matmul(ps[:, 4 * c + n, :], h, wlo[:, s, n * 512:(n + 1) * 512], start=False, stop=False,
                              skip_group_check=True)
                for n in range(4):
                    mm = pe.matmul(ps[:, 4 * c + n, :], l, whi[:, s, n * 512:(n + 1) * 512], start=False, stop=last,
                                   skip_group_check=True)
            return mm

        def stage_hi(act, src, m0, mpr, jm, i):
            if not isinstance(i, int) or i * mpr + m0 + jm >= 2:
                act.wait_ge(w_used, i * mpr + (m0 + jm - 1))
            act.activation(shi[:, (m0 + jm) % 2, :], src, ACT.Identity)

        def stage_lo(dve, src, m0, mpr, jm, i):
            dve.wait_ge(hi_ready, i * mpr + (m0 + jm + 1))
            dve.tensor_tensor(slo[:, (m0 + jm) % 2, :], src, shi[:, (m0 + jm) % 2, :].bitcast(F32), ALU.subtract)

        def newton(ch, dve, y, x, t):
            ch.link(dve.tensor_scalar(y.bitcast(I32), x.bitcast(I32), -0.5, RSQRT_SEED, ALU.mult, ALU.add))
            for _ in range(3):
                ch.link(dve.tensor_tensor(t, y, y, ALU.mult))
                ch.link(dve.scalar_tensor_tensor(out=t, in0=t, scalar=-0.5, in1=x, op0=ALU.mult, op1=ALU.mult))
                ch.link(dve.scalar_tensor_tensor(out=y, in0=t, scalar=1.5, in1=y, op0=ALU.add, op1=ALU.mult))

        def bc(v, n):
            return v.unsqueeze(2).to_broadcast([P, v.shape[1], n])

        def rep(v, n):
            return v.unsqueeze(1).to_broadcast([P, n, v.shape[1]])

        def norm_col(which, layer):
            at = (which * 2 + layer) * KT
            return normc[:, at:at + KT]

        SUB = [dict(layer=s // 2, pre=0 if s % 2 == 0 else 2, post=1 if s % 2 == 0 else 3,
                    sh=0 if s % 2 == 0 else 3, sc=1 if s % 2 == 0 else 4, gt=2 if s % 2 == 0 else 5)
               for s in range(4)]
        gwrow_of = [gwrow_mix, gwrow_ffn, gwrow_mix, gwrow_ffn]

        def mod_cols(layer, chunk):
            return modc[:, layer, chunk * KT:(chunk + 1) * KT]

        FINALS = [(0, [0, 1], macc), (0, [2, 3], macc), (0, [4, 5], macc), (1, [0, 1, 2, 3], macc4),
                  (1, [4, 5], macc4)]
        H_HI = [0, 4, 8, 14]
        mod_ends = [n_ab, n_dout, n_gu0, n_dn0, n_sin]

        block = ctx.enter_context(nc.Block())

        @block.sync
        def _(sp):
            rows = pin
            sp.dma_start(xbuf, a["x"][0].rearrange("(c p) n -> p c n", p=P)).then_inc(x_landed, 16)
            for n, name in enumerate(("norm_pre_mix", "norm_post_mix", "norm_pre_ffn", "norm_post_ffn")):
                sp.dma_start(rows[32 * n:32 * n + 32, 0, :],
                             a[name].rearrange("l (k p) -> (l k) p", p=P)).then_inc(params_in, 16)
            mb = a["mod_b"].rearrange("l (k p) -> (l k) p", p=P)
            sp.dma_start(rows[0:96, 1, :], mb[0:96, :]).then_inc(params_in, 16)
            sp.dma_start(rows[0:96, 2, :], mb[96:192, :]).then_inc(params_in, 16)
            sp.dma_start(rows[0:16, 3, :], a["c"].rearrange("b (k p) -> (b k) p", p=P)).then_inc(params_in, 16)
            sp.dma_start(rows[16:32, 3, :], a["s5_d"].rearrange("b (k p) -> (b k) p", p=P)).then_inc(params_in, 16)
            sp.dma_start(rows[32:33, 3, :], a["dn_norm_w"]).then_inc(params_in, 16)
            cw = a["dn_conv_w"].rearrange("l j (t p) -> (l j t) p", p=P)
            sp.dma_start(rows[:, 4, :], cw[0:128, :]).then_inc(params_in, 16)
            sp.dma_start(rows[:, 5, :], cw[128:256, :]).then_inc(params_in, 16)
            sp.dma_start(rows[0:64, 6, :], cw[256:320, :]).then_inc(params_in, 16)
            sp.wait_ge(consts_ready, 1)
            for d in range(2):
                r = 64 * d + 32
                sp.dma_start(small[r:r + 32, 0:1], a["dn_a_log"][0, d, :].rearrange("(h o) -> h o", o=1)).then_inc(params_in, 16)
                sp.dma_start(small[r:r + 32, 1:2], a["dn_dt_bias"][0, d, :].rearrange("(h o) -> h o", o=1)).then_inc(params_in, 16)
            for j in range(2):
                load_mod(sp, 0, 0, 2, j, 0, 0, j)
            with sp.Fori(0, KT - 1) as k:
                for j in range(2):
                    load_mod(sp, 2, k, 2, j, 0, k + 1, j)
            w_in = a["dn_w_in"][0]
            load_cols(sp, n_ab, 0, 1, 0, w_in, 0, KT, ABOFF, P)

            def head_tiles(h):
                load_cols(sp, n_head, h, PER_HEAD, 0, w_in, 0, KT, QOFF + h * P, P)
                load_cols(sp, n_head, h, PER_HEAD, 1, w_in, 0, KT, KOFF + h * P, P)
                for j in range(2):
                    load_cols(sp, n_head, h, PER_HEAD, 2 + j, w_in, 8 * j, 8, VOFF + h * 256, 256)
                for j in range(2):
                    load_cols(sp, n_head, h, PER_HEAD, 4 + j, w_in, 8 * j, 8, ZOFF + h * 256, 256)
                for j in range(2):
                    load_mod(sp, n_head, h, PER_HEAD, 6 + j, 0, h, 2 + j)

            with sp.Fori(0, KH) as h:
                head_tiles(h)
            def load_x(s):
                src = a["x"][0] if s == 0 else x_dram[s - 1]
                sp.wait_ge(w_used, post_m[s])
                if s > 0:
                    sp.wait_ge(x_stored, 16 * s)
                sp.dma_start(xbuf, src.rearrange("(c p) n -> p c n", p=P)).then_inc(x_landed, 16)

            def store_x(s):
                sp.wait_ge(x_new, 2 * s + 2)
                dst = out[0] if s == 3 else x_dram[s]
                sp.dma_start(dst.rearrange("(c p) n -> p c n", p=P), xbuf).then_inc(x_stored, 16)

            def gateup(n0, layer, loops):
                wg, wu = a["ffn_w_gate"][layer], a["ffn_w_up"][layer]
                lm, lp = loops

                def pair(nb, i, per, j0, col, k=None):
                    for w, j in ((wg, 0), (wg, 1), (wu, 2), (wu, 3)):
                        load_cols(sp, nb, i, per, j0 + w_at(per == 16, j), w, 8 * (j % 2), 8, col, 256)
                        if per == 16:
                            load_mod(sp, nb, i, per, j0 + 2 * j + 1, 1, k, j)

                if lm:
                    with sp.Fori(0, lm) as i:
                        for r in range(2):
                            pair(n0, i, 16, 8 * r, i * 512 + r * 256, i * 2 + r)
                n1 = n0 + 16 * lm
                with sp.Fori(0, lp) as i:
                    for r in range(2):
                        pair(n1, i, 8, 4 * r, i * 512 + (r * 256 + lm * 512))

            def down(n0, w, kts, lm, layer):
                if lm:
                    with sp.Fori(0, lm) as i:
                        for j in range(4):
                            load_rows(sp, n0, i, 8, 2 * j, w, i * (4 * P) + j * P)
                            load_mod(sp, n0, i, 8, 2 * j + 1, layer, i * 2 + j // 2, 4 + j % 2)
                n1 = n0 + 8 * lm
                if kts // 4 > lm:
                    with sp.Fori(0, kts // 4 - lm) as i:
                        for j in range(4):
                            load_rows(sp, n1, i, 4, j, w, i * (4 * P) + (j + 4 * lm) * P)

            sp.wait_ge(raw_used, n_dout)
            sp.wait_ge(oT_ready, KH)
            down(n_dout, a["dn_w_out"][0], VH, LOOPM, 0)
            load_x(0)
            store_x(0)
            gateup(n_gu0, 0, (LOOPM, 3))
            down(n_dn0, a["ffn_w_down"][0], FT, LOOPM, 1)
            load_x(1)
            store_x(1)

            def square(n0, w):
                with sp.Fori(0, 4) as i:
                    for r in range(2):
                        for j in range(2):
                            load_cols(sp, n0, i, 4, 2 * r + j, w, 8 * j, 8, i * 512 + r * 256, 256)

            square(n_sin, a["s5_w_in"][0])
            sp.wait_ge(h_ready, 3)
            sp.wait_ge(mod_ps, 5)
            for r, name in enumerate(("s5_b_re", "s5_b_im")):
                for d in range(2):
                    sp.dma_start(bnat[:, r, d * GP * Q:(d + 1) * GP * Q].rearrange("p (g c) -> p g c", c=Q),
                                 a[name][0, d].rearrange("(g e) p c -> (e p) g c", e=2)).then_inc(s5_in, 16)
            for r, name in enumerate(("s5_c_re", "s5_c_im")):
                for d in range(2):
                    sp.dma_start(cnat[:, r, d, :, :],
                                 a[name][0, d].rearrange("(j g) c p -> (g c) j p", g=8)).then_inc(s5_in, 16)
            sp.dma_start(s5w[:, 0, :], a["s5_lam_re"][0].rearrange("d (g e) p -> (d g) (e p)", e=2)).then_inc(s5_in, 16)
            sp.dma_start(s5w[:, 1, :], a["s5_lam_im"][0].rearrange("d (g e) p -> (d g) (e p)", e=2)).then_inc(s5_in, 16)
            sp.dma_start(s5w[:, 2, 0:2], a["s5_log_step"][0].rearrange("d (g e) -> (d g) e", e=2)).then_inc(s5_in, 16)
            sp.wait_ge(ysum_ready, NJ + 1)
            square(n_glu, a["s5_w_glu"][0])
            down(n_sout, a["s5_w_out"][0], KT, 0, 1)
            load_x(2)
            store_x(2)
            gateup(n_gu1, 1, (0, 11))
            down(n_dn1, a["ffn_w_down"][1], FT, 0, 1)
            load_x(3)
            store_x(3)
            sp.wait_ge(x_stored, 64)


        QK_BANK, V_BANK, Z_BANK, K_BANK, XY, TT = 0, 1, 2, 3, (4, 5), (6, 7)

        def changed(v, l, d):
            return v.rearrange("p u (n t b) -> p u n t b", t=2, b=2 << l)[:, :, :, d, :]

        def at_level(h, l, d):
            return h * (2 * LV) + (2 * l + d + 1)

        def plan(n0, m0, kts, lm):
            out_, i, its = [], 0, kts // 4
            while i < its:
                per = 8 if i < lm else 4
                end = i + 1 if i in (0, its - 1) else (min(lm, its - 1) if i < lm else its - 1)
                out_.append((n0, m0 + 4 * i, 4 * i, end - i, per, i == 0, end == its))
                n0 += per * (end - i)
                i = end
            return out_

        def run(eng, trips, body):
            if trips == 1:
                body(0)
            else:
                with eng.Fori(0, trips) as i:
                    body(i)

        @block.tensor
        def _(pe):
            def finish_mod(f):
                layer, chunks, acc = FINALS[f]
                pe.wait_ge(raw_used, mod_ends[f])
                for n in range(len(chunks)):
                    for k in range(KT):
                        mm = pe.matmul(ps[:, 7, n * KT + k:n * KT + k + 1], acc[:, n, k * P:(k + 1) * P],
                                       ones[:, 0:1], start=True, stop=True)
                mm.then_inc(mod_ps, 1)

            def pre_norm(s):
                pe.wait_ge(xn_ready, 2 * s + 2)
                for k in range(KT):
                    for c in range(NT):
                        mm = pe.transpose(ps[:, k // 2, (k % 2) * T + c * P:(k % 2) * T + (c + 1) * P],
                                          xn[:, c, k * P:(k + 1) * P], ident)
                    if k % 2:
                        mm.then_inc(xnT_ps, 1)

            def token_major(n0, m0, kts, lm):
                for nb, mb, _, trips, per, first, last in plan(n0, m0, kts, lm):
                    def body(i):
                        for j in range(4):
                            split_ready(pe, nb, per, w_at(per == 8, j), mb, 4, j, i)
                            tm_pass(pe, (mb + j) % 2, (mb + j) % 2, first and j == 0,
                                    last and j == 3).then_inc(w_used, 1)
                    run(pe, trips, body)

            def half_tile(h, k, prev):
                j, half = k // 2, k % 2
                s = (m_head + j) % 2
                if half == 0:
                    split_ready(pe, n_head, PER_HEAD, j, m_head, 6, j, h)
                if j < 2:
                    if k == 0 and prev:
                        pe.wait_ge(cbuf_ready, h * 2 - 1)
                    mm = fm_block(pe, ps[:, QK_BANK, j * T:(j + 1) * T], s, half * 8 * P, P, 8, 8 * half,
                                  half == 0, half == 1)
                elif j < 4:
                    if k == 4 and prev:
                        pe.wait_ge(cbuf_ready, h * 2)
                    mm = fm_block(pe, ps[:, V_BANK, half * T:(half + 1) * T], s, half * P, 2 * P, 8, 8 * (j - 2),
                                  j == 2 and half == 0, j == 3)
                else:
                    if k == 8 and prev:
                        pe.wait_ge(zg_ready, h)
                    for kt in range(8):
                        kk = 8 * (j - 4) + kt
                        mm = three(pe, ps[:, Z_BANK, half * T:(half + 1) * T],
                                   hhi[:, kk, half * P:(half + 1) * P], hlo[:, kk, half * P:(half + 1) * P],
                                   whi[:, s, kt * 2 * P:(kt + 1) * 2 * P], wlo[:, s, kt * 2 * P:(kt + 1) * 2 * P],
                                   j == 4 and half == 0 and kt == 0, j == 5 and kt == 7)
                if half == 1:
                    mm.then_inc(w_used, 1)

            def core(h, nxt):
                for k in range(5):
                    nxt(k)
                pe.wait_ge(act_done, h + 1)
                for u in range(4):
                    pe.transpose(ps[:, TT[0], u * P:(u + 1) * P], yact[:, u * P:(u + 1) * P], ident)
                for u in range(4):
                    mm = pe.transpose(ps[:, TT[1], u * P:(u + 1) * P], yact[:, (4 + u) * P:(5 + u) * P], ident)
                mm.then_inc(tok_ps, 1)
                for k in range(5, 8):
                    nxt(k)
                pe.wait_ge(qkn_ready, h + 1)
                for u in range(4):
                    mm = pe.transpose(ps[:, XY[0], u * P:(u + 1) * P], qkn[:, u, :], ident)
                mm.then_inc(qkT_ps, 1)
                pe.wait_ge(qkT_ready, h + 1)
                for m in range(2):
                    for c in range(NT):
                        mm = pe.matmul(ps[:, K_BANK, (2 * m + c) * P:(2 * m + c + 1) * P], qkT[:, 2 + c, :],
                                       qkT[:, 2 - 2 * m + c, :], start=True, stop=True)
                mm.then_inc(kk_ps, 1)
                nxt(8)
                nxt(9)
                for d in range(2):
                    pe.wait_ge(s0_ready, h * 2 + (d + 1))
                    pe.wait_ge(vb_ready, h + 1)
                    for u in range(4):
                        mm = pe.transpose(ps[:, TT[d], u * P:(u + 1) * P], Sm[:, 4 * d + u, :], ident)
                    mm.then_inc(t0_ps, 1)
                for l in range(LV):
                    for d in range(2):
                        if l == 0:
                            pe.wait_ge(t0_ready, h * 2 + (d + 1))
                        else:
                            pe.wait_ge(t_ready, at_level(h, l - 1, d))
                        for u in range(4):
                            mm = pe.matmul(ps[:, XY[d], u * 64:(u + 1) * 64], Bm[:, 4 * d + u, :],
                                           changed(Tm[:, 4 * d + u:4 * d + u + 1, :], l, d)[:, 0],
                                           start=True, stop=True)
                        mm.then_inc(x_ps, 1)
                    for d in range(2):
                        pe.wait_ge(xm_ready, at_level(h, l, d))
                        if l > 0:
                            pe.wait_ge(s_ready, at_level(h, l - 1, d))
                        for u in range(4):
                            mm = pe.matmul(ps[:, XY[d], 256 + u * 64:256 + (u + 1) * 64], Sm[:, 4 * d + u, :],
                                           Xm[:, d, u, :], start=True, stop=True)
                        mm.then_inc(y_ps, 1)
                    for d in range(2):
                        pe.wait_ge(t_ready, at_level(h, l, d))
                        for u in range(4):
                            mm = pe.transpose(ps[:, TT[d], u * P:(u + 1) * P], Tm[:, 4 * d + u, :], ident)
                        mm.then_inc(tt_ps, 1)
                for d in range(2):
                    pe.wait_ge(s_ready, at_level(h, LV - 1, d))
                    for v in range(2):
                        mm = pe.matmul(ps[:, XY[d], v * P:(v + 1) * P], Sm[:, 4 * d + 2 * v + d, :],
                                       Vb[:, 4 * d + 2 * v + d, :], start=True, stop=True)
                    mm.then_inc(u0_ps, 1)
                pe.wait_ge(ktail_ready, h + 1)
                for d in range(2):
                    pe.wait_ge(u0_ready, h * 2 + (d + 1))
                    for v in range(2):
                        mm = pe.matmul(ps[:, TT[d], v * P:(v + 1) * P], Kt[:, d, v, :],
                                       Vn[:, 4 * d + 2 * v + d, :], start=True, stop=True)
                    mm.then_inc(st_ps, 1)
                for d in range(2):
                    pe.wait_ge(st_ready, h * 2 + (d + 1))
                    state = Ssb[:, d, :, :].rearrange("p v i -> p (v i)")
                    pe.matmul(ps[:, XY[d], 256:512], qkT[:, 3 - d, :], state, start=True, stop=True)\
                        .then_inc(ks_ps, 1)
                    pe.matmul(ps[:, TT[d], 256:512], qkT[:, 1 - d, :], state, start=True, stop=True)\
                        .then_inc(ks_ps, 1)
                for d in range(2):
                    pe.wait_ge(r1_ready, h * 2 + (d + 1))
                    for v in range(2):
                        mm = pe.matmul(ps[:, XY[d], v * P:(v + 1) * P], Sm[:, 4 * d + 2 * v + 1 - d, :],
                                       R1[:, d, v, :], start=True, stop=True)
                    mm.then_inc(v1_ps, 1)
                pe.wait_ge(aqk_ready, h * 2 + 2)
                pe.wait_ge(v1_ready, h * 2 + 2)
                for u in range(4):
                    for d in range(2):
                        mm = pe.matmul(ps[:, K_BANK, u * P:(u + 1) * P], Aqk[:, 4 * d + u, :], Vn[:, 4 * d + u, :],
                                       start=d == 0, stop=d == 1)
                mm.then_inc(o_ps, 1)
                nxt(10)
                nxt(11)
                pe.wait_ge(og_ready, h + 1)
                for u in range(4):
                    mm = pe.transpose(ps[:, TT[0], u * P:(u + 1) * P], Osb[:, u, :], ident)
                mm.then_inc(oT_ps, 1)

            def pair_gemm(nb, nper, jn, mb, mper, jm, i, bank, mods=False):
                for j in range(2):
                    split_ready(pe, nb, nper, jn + w_at(mods, j), mb, mper, jm + j, i)
                    for b in range(2):
                        mm = fm_block(pe, ps[:, bank, b * T:(b + 1) * T], (mb + jm + j) % 2, b * P, 2 * P, 8, 8 * j,
                                      j == 0 and b == 0, j == 1)
                    mm.then_inc(w_used, 1)

            def gateup(n0, m0, q0, lm, lp):
                def pairs(i, nb, nper, mb, q):
                    for r in range(2):
                        jn = (nper // 2) * r
                        pe.wait_ge(gate_used, i * 2 + (q + r + 1))
                        pair_gemm(nb, nper, jn, mb, 8, 4 * r, i, r, nper == 16)
                        pe.wait_ge(hid_ready, i * 2 + (q + r + 1))
                        pair_gemm(nb, nper, jn + w_at(nper == 16, 2), mb, 8, 4 * r + 2, i, 2 + r, nper == 16)
                if lm:
                    with pe.Fori(0, lm) as i:
                        pairs(i, n0, 16, m0, q0)
                with pe.Fori(0, lp) as i:
                    pairs(i, n0 + 16 * lm, 8, m0 + 8 * lm, q0 + 2 * lm)

            def square(n0, m0, q0):
                with pe.Fori(0, 4) as i:
                    for r in range(2):
                        pe.wait_ge(fm_done, i * 2 + (q0 + r + 1))
                        pair_gemm(n0, 4, 2 * r, m0, 4, 2 * r, i, r)

            for free, n in ((o_ps, 1), (ymm, 2), (bcT_ps, 1), (bu_ps, 1)):
                pe.sem_inc(free, n)
            pe.wait_ge(consts_ready, 3)
            pe.wait_ge(params_in, 16 * 16)
            for n, rows in enumerate((128, 96, 96, 33, 128, 128, 64)):
                mm = pe.transpose(ps[:, n // 4, (n % 4) * P:(n % 4) * P + rows], pin[0:rows, n, :],
                                  ident[0:rows, 0:rows])
            mm.then_inc(params_T, 1)
            finish_mod(0)
            pe.wait_ge(mod_ready, 1)
            pre_norm(0)
            pe.wait_ge(h_ready, 1)
            split_ready(pe, n_ab, 1, 0, m_ab, 1, 0, 0)
            fm_block(pe, ps[:, 4, 0:T], m_ab % 2, 0, P, KT, 0, True, True).then_inc(w_used, 1)
            pe.wait_ge(ab_dve, 3)
            for n in range(4):
                src = abw[:, 1 if n < 2 else 2, (n % 2) * P:(n % 2 + 1) * P]
                mm = pe.transpose(ps[:, 5, n * P:(n + 1) * P], src, ident)
            mm.then_inc(gT_ps, 1)
            pe.wait_ge(tbl_ready, 1)
            for k in range(12):
                half_tile(0, k, False)
            with pe.Fori(0, KH - 1) as h:
                core(h, lambda k: half_tile(h + 1, k, True))
            finish_mod(1)
            pe.wait_ge(mod_ready, 2)
            core(KH - 1, lambda k: None)
            pe.wait_ge(oT_ready, KH)
            token_major(n_dout, m_dout, VH, LOOPM)
            pe.wait_ge(x_new, 2)
            finish_mod(2)
            pe.wait_ge(mod_ready, 3)
            pre_norm(1)
            pe.wait_ge(h_ready, 2)
            gateup(n_gu0, m_gu0, 0, LOOPM, 3)
            finish_mod(3)
            pe.wait_ge(mod_ready, 4)
            pe.wait_ge(hid_ready, 2 + FT // 2)
            token_major(n_dn0, m_dn0, FT, LOOPM)
            pe.wait_ge(x_new, 4)
            finish_mod(4)
            pe.wait_ge(mod_ready, 5)
            pre_norm(2)
            pe.wait_ge(h_ready, 3)
            square(n_sin, m_sin, 0)

            pe.wait_ge(s5_dve, 1)
            for n in range(4):
                mm = pe.transpose(ps[:, 2, n * P:(n + 1) * P], s5w[:, S5OUT[n], :], ident)
            mm.then_inc(s5_psT, 1)
            pe.wait_ge(fm_done, 2 + 8)

            def transposes(j):
                pe.wait_ge(bx_ready, j + 1)
                pe.wait_ge(bT_ready, j + 1)
                for n in range(4):
                    pe.transpose(ps[:, 0, n * P:(n + 1) * P], bx[:, n, :], ident)
                pe.wait_ge(cdup_ready, j + 1)
                pe.wait_ge(cj_ready, j + 1)
                for n in range(4):
                    mm = pe.transpose(ps[:, 1, n * P:(n + 1) * P], cdup[:, n, :], ident)
                mm.then_inc(bcT_ps, 1)

            def bu(j, q, first=False):
                g, d = q // 2, q % 2
                if q == 0:
                    pe.wait_ge(bT_ready, j + 2)
                if not first:
                    pe.wait_ge(t_prod, j * 8 + (q - 1))
                for r in range(2):
                    mm = pe.matmul(ps[:, 2 + q % 2, r * T:(r + 1) * T], bT[32 * g:32 * g + 32, 2 * d + r, :],
                                   uj[32 * g:32 * g + 32, :], start=True, stop=True)
                mm.then_inc(bu_ps, 1)

            def y(j, q):
                g, d = q // 2, q % 2
                if q == 0:
                    pe.wait_ge(cj_ready, j + 2)
                    pe.wait_ge(ysum_ready, j + 1)
                o = ps[32 * g:32 * g + 32, 4, 0:T]
                pe.wait_ge(pcos_ready, j * 8 + (q + 5))
                for r in range(2):
                    pe.matmul(o, cj[:, r, (2 * d + r) * P + 32 * g:(2 * d + r) * P + 32 * g + 32], pcos[:, q % 2, r, :],
                              start=d == 0 and r == 0, stop=False)
                pe.wait_ge(psin_ready, j * 8 + (q + 5))
                for r in range(2):
                    mm = pe.matmul(o, cj[:, 1 - r, (2 * d + r) * P + 32 * g:(2 * d + r) * P + 32 * g + 32],
                                   psin[:, q % 2, r, :], start=False, stop=d == 1 and r == 1)
                mm.then_inc(ymm, 1)

            def s5_tile(j, more):
                for q in range(2, 8):
                    bu(j, q)
                    y(j, q - 2)
                if more:
                    transposes(j + 1)
                y(j, 6)
                if more:
                    bu(j + 1, 0)
                y(j, 7)
                if more:
                    bu(j + 1, 1)

            pe.wait_ge(s5_ready, 1)
            transposes(0)
            bu(0, 0, True)
            bu(0, 1, True)
            with pe.Fori(0, NJ - 1) as j:
                s5_tile(j, True)
            s5_tile(NJ - 1, False)
            pe.wait_ge(glu_h, 2)
            square(n_glu, m_glu, 8)
            pe.wait_ge(fm_done, 2 + 16)
            token_major(n_sout, m_sout, KT, 0)
            pe.wait_ge(x_new, 6)
            pre_norm(3)
            pe.wait_ge(h_ready, 4)
            gateup(n_gu1, m_gu1, FT // 2, 0, FT // 4)
            pe.wait_ge(hid_ready, 2 + FT)
            token_major(n_dn1, m_dn1, FT, 0)

        @block.gpsimd
        def _(pool):
            ch = Chain(pool, pools)

            def select(view, pattern, base, cm, op=ALU.is_ge, fill=0.0):
                ch.link(pool.affine_select(out=view, in_=view, compare_op=op, fill=fill, base=base,
                                           pattern=pattern, channel_multiplier=cm))

            pool.sem_inc(psin_ready, 4)
            pool.memset(small, 0.0).then_inc(consts_ready, 1)
            ch.link(pool.memset(ones, 1.0))
            ch.link(pool.memset(ident, 0.0))
            select(ident, [[-1, P]], 0, 1, ALU.not_equal, 1.0)
            pool.wait_ge(pools, 3)
            pool.memset(macc, 0.0).then_inc(macc_zero, 1)
            ch.link(pool.memset(mkq[:, :, 0, :], 1.0))
            ch.link(pool.memset(mkq[:, :, 1, :], DK_SCALE))
            for d in range(2):
                sg = 1 if d == 0 else -1
                select(mkq[:, d, 0, :], [[sg, P]], -1, -sg)
                select(mkq[:, d, 1, :], [[sg, P]], 0, -sg)
            ch.link(pool.memset(m1, 0.0))
            for d in range(2):
                v = m1[:, d, :].rearrange("p (a r) -> p a r", r=2)[:, :, 1 - d]
                select(v, [[-2, P // 2]], -d, 1, ALU.not_equal, -1.0)
            ch.link(pool.memset(mlv, -1.0))
            for l in range(LV):
                b = 2 << l
                for d in range(2):
                    v = mlv[:, l, d, :].rearrange("p (n b) -> p n b", b=b)
                    select(v, [[-2 * b, 64 // b], [0, b]], -(1 - d) * b, 1)
                    select(v, [[2 * b, 64 // b], [0, b]], (2 - d) * b - 1, -1)
            pool.sem_inc(consts_ready, 2)
            pool.wait_ge(ab_dve, 3)
            for d in range(2):
                pool.dma_start(g_rows[d * VH:(d + 1) * VH, :], abw[64 * d + 32:64 * d + 64, 1, :]).then_inc(rows_stored, 16)
                pool.dma_start(b_rows[d * VH:(d + 1) * VH, :], abw[64 * d:64 * d + 32, 2, :]).then_inc(rows_stored, 16)
            pool.wait_ge(mod_ps, 1)
            pool.wait_ge(h_ready, 1)
            pool.memset(macc, 0.0).then_inc(macc_zero, 1)
            pool.wait_ge(rows_stored, 64)

            def core(h, later):
                if later:
                    pool.wait_ge(oss_ready, h + 1)
                    pool.wait_ge(og_ready, h)
                    pool.wait_ge(oT_ps, h)
                for d in range(2):
                    for dst, src in ((grow, g_rows), (brow, b_rows)):
                        pool.dma_start(dst[:, 4 * d:4 * d + 4, :].rearrange("p (v c) i -> p v (c i)", v=2),
                                       src[ds(h * 2 + d * VH, 2), :].partition_broadcast(P)).then_inc(rows_landed, 16)
                if later:
                    pool.wait_ge(tt_ps, h * (2 * LV))
                for d in range(2):
                    pool.wait_ge(e_ready, h * 2 + (d + 1))
                    pool.wait_ge(rows_landed, h * 64 + 64)
                    pool.tensor_tensor(Bm[:, 4 * d:4 * d + 4, :], eD[:, d * 512:(d + 1) * 512].rearrange("p (u i) -> p u i", u=4),
                                       brow[:, 4 * d:4 * d + 4, :], ALU.mult).then_inc(eb_ready, 1)
                for d in range(2):
                    pool.wait_ge(km_ready, h + 1)
                    for v in range(2):
                        mm = pool.tensor_tensor(Aqk[:, 4 * d + 2 * v:4 * d + 2 * v + 2, :], km[:, d, 1, :, :],
                                                eD[:, d * 512 + v * 256:d * 512 + (v + 1) * 256].rearrange("p (u i) -> p u i", u=2),
                                                ALU.mult)
                    mm.then_inc(aqk_ready, 1)

            core(0, False)
            with pool.Fori(0, KH - 1) as h:
                core(h + 1, True)
            pool.wait_ge(mod_ps, 2)
            pool.memset(macc, 0.0).then_inc(macc_zero, 1)

            def gate_row(s):
                pool.wait_ge(gw_col, s + 1)
                pool.dma_start(gw_rows[s, :].rearrange("(k p) -> p k", p=P), gwcol[:, s, :],
                               allow_slow_non_contiguous=True).then_inc(gw_stored, 16)
                pool.wait_ge(gw_stored, 16 * s + 16)
                pool.dma_start(gwrow_of[s], gw_rows[s:s + 1, :].partition_broadcast(P).rearrange("p o n -> p (o n)"))\
                    .then_inc(gw_landed, 16)

            pool.wait_ge(oT_ready, KH)
            gate_row(0)
            pool.wait_ge(x_new, 2)
            gate_row(1)
            pool.wait_ge(mod_ps, 3)
            pool.memset(macc4, 0.0).then_inc(macc_zero, 1)
            pool.wait_ge(mod_ps, 4)
            pool.memset(macc4[:, 0:2, :], 0.0).then_inc(macc_zero, 1)

            pool.wait_ge(s5_ready, 1)
            ch.link(pool.memset(gmask, 0.0))
            for sgn in range(2):
                for e in range(2):
                    v = gmask[64 * e:64 * e + 64, sgn, :].rearrange("p (g e c) -> p g e c", g=4, e=2)[:, :, e, :]
                    ch.link(pool.memset(v, 1.0 if sgn == 0 else -1.0))
            ch.link(pool.iota(iota, pattern=[[1, T]], base=0, channel_multiplier=0,
                              allow_small_or_imprecise_dtypes=True))
            pool.sem_inc(s5_act, 1)

            def operands(j):
                pool.wait_ge(bcT_ps, j + 1)
                for n in range(4):
                    d, r = n // 2, n % 2
                    src = bnat[:, r, :].rearrange("p (g c) -> p g c", c=Q)[:, ds(j * 4 + d * GP, 4), :]
                    m = pool.tensor_tensor(bx[:, n, :].rearrange("p (g e c) -> p g e c", g=4, e=2),
                                           src.unsqueeze(2).to_broadcast([P, 4, 2, Q]),
                                           gmask[:, 0, :].rearrange("p (g e c) -> p g e c", g=4, e=2), ALU.mult)
                m.then_inc(bx_ready, 1)
                for n in range(4):
                    d, r = n // 2, n % 2
                    for e in range(2):
                        m = pool.tensor_copy(cdup[:, n, e * 64:(e + 1) * 64],
                                             cnat[:, r, d, ds(j, 1), :].rearrange("p o s -> p (o s)"))
                m.then_inc(cdup_ready, 1)

            def s5_tile(j, more):
                def add(q):
                    pool.wait_ge(t_prod, j * 8 + (q + 1))
                    pool.wait_ge(z_ready, j * 8 + (q + 1))
                    pool.tensor_tensor(zin[:, q % 2], tprod[:, q % 2, 0], tprod[:, q % 2, 1],
                                       ALU.add).then_inc(zin_ready, 1)

                add(0)
                for q in range(8):
                    if q < 7:
                        add(q + 1)
                    pool.wait_ge(z_ready, j * 8 + (q + 3))
                    pool.wait_ge(ymm, j * 8 + (q + 1))
                    pool.tensor_tensor(psin[:, q % 2], trig[:, q % 4, 1:3, :], zst[:, q % 2, ::-1, :],
                                       ALU.mult).then_inc(psin_ready, 1)
                    if q == 3 and more:
                        operands(j + 1)

            operands(0)
            with pool.Fori(0, NJ - 1) as j:
                s5_tile(j, True)
            s5_tile(NJ - 1, False)
            pool.wait_ge(ysum_ready, NJ + 1)
            gate_row(2)
            pool.wait_ge(x_new, 6)
            gate_row(3)

        @block.scalar
        def _(act):
            ch = Chain(act, acts)
            IDT = ACT.Identity

            def post(s):
                act.wait_ge(w_used, post_m[s])
                for n in range(8):
                    m = act.activation(ptmp[:, n // 4, n % 4 * 512:(n % 4 + 1) * 512], ps[:, n, :], ACT.Square, accum_out=small[:, 8 + n:9 + n])
                m.then_inc(ss_out, 1)

            def pre_norm(s):
                if s == 0:
                    act.wait_ge(x_landed, 16)
                for c in range(NT):
                    if s > 0:
                        act.wait_ge(x_new, 2 * s - 1 + c)
                    m = act.activation(xn[:, c, :], xbuf[:, c, :], ACT.Square, accum_out=small[:, 24 + c:25 + c])
                m.then_inc(ss_x, 1)
                act.wait_ge(rstd_x, s + 1)
                act.activation(xn[:, 0, :], xbuf[:, 0, :], IDT, scale=small[:, 28:29]).then_inc(xn_ready, 1)
                layer, sh = SUB[s]["layer"], SUB[s]["sh"]
                for b in range(0, KT // 2, 2):
                    act.wait_ge(xnT_ps, 8 * s + b + 1)
                    for k in (2 * b, 2 * b + 1):
                        m = act.activation(hfull[k // 4][:, k % 4, :], ps[:, b, (k % 2) * T:(k % 2 + 1) * T], IDT,
                                           scale=acol[:, k:k + 1], bias=mod_cols(layer, sh)[:, k:k + 1])
                m.then_inc(h_act, 1)
                act.wait_ge(h_act, s + 1)
                act.wait_ge(h_dve, s + 1)
                for q in range(4):
                    k4 = slice(4 * q, 4 * q + 4)
                    act.activation(hhi[:, k4, :], hfull[q], IDT).then_inc(h_hi, 1)

            def stream(n0, m0, kts, lm, src):
                for nb, mb, kb_, trips, per, first, last in plan(n0, m0, kts, lm):
                    def body(i):
                        for j in range(4):
                            stage_hi(act, src[:, ds(i * 4 + (kb_ + j), 1), :].rearrange("p o t -> p (o t)"),
                                     mb, 4, j, i)
                            split_hi(act, nb, per, w_at(per == 8, j), mb, 4, j, i)
                    run(act, trips, body)

            def gate_tanh_of(q, r, m_done):
                act.wait_ge(w_used, m_done)
                act.wait_ge(hid_ready, q + 1)
                act.activation(fth[:, r, :], ps[:, r, :], ACT.Tanh, scale=0.5).then_inc(gate_tanh, 1)

            def gateup(n0, m0, q0, lm, lp):
                def pairs(i, nb, nper, mb, q):
                    for r in range(2):
                        jn = (nper // 2) * r
                        for j in range(4):
                            split_hi(act, nb, nper, jn + w_at(nper == 16, j), mb, 8, 4 * r + j, i)
                            if j == 3:
                                gate_tanh_of(i * 2 + (q + r), r, i * 8 + (mb + 4 * r + 2))
                if lm:
                    with act.Fori(0, lm) as i:
                        pairs(i, n0, 16, m0, q0)
                with act.Fori(0, lp) as i:
                    pairs(i, n0 + 16 * lm, 8, m0 + 8 * lm, q0 + 2 * lm)

            def head_hi(h, j):
                split_hi(act, n_head, PER_HEAD, j, m_head, 6, j, h)

            def conv_inputs(h):
                act.wait_ge(w_used, h * 6 + (m_head + 2))
                act.wait_ge(o_ps, h + 1)
                for edge in (slice(0, PAD), slice(PAD + T, 2 * PAD + T)):
                    act.activation(cbuf[:, :, edge], ones[:, 0:4 * PAD].rearrange("p (t n) -> p t n", t=4), IDT,
                                   scale=0.0)
                act.activation(cbuf[:, 0:2, PAD:PAD + T], ps[:, QK_BANK, :].rearrange("p (t n) -> p t n", t=2),
                               IDT).then_inc(cbuf_ready, 1)
                act.wait_ge(w_used, h * 6 + (m_head + 4))
                act.activation(cbuf[:, 2:4, PAD:PAD + T], ps[:, V_BANK, :].rearrange("p (t n) -> p t n", t=2),
                               IDT).then_inc(cbuf_ready, 1)

            def core(h, nxt, more=True):
                nxt(1)
                nxt(2)
                act.wait_ge(conv_done, h + 1)
                act.activation(eD, yact, ACT.Tanh, scale=0.5).then_inc(silu_tanh, 1)
                act.wait_ge(w_used, h * 6 + (m_head + 6))
                act.activation(zth.rearrange("p u i -> p (u i)"), ps[:, Z_BANK, :], ACT.Tanh, scale=0.5).then_inc(z_tanh, 1)
                nxt(3)
                act.wait_ge(tok_ps, h + 1)
                act.wait_ge(oss_ready, h + 1)
                for u in range(4):
                    m = act.activation(junk[:, u * P:(u + 1) * P], ps[:, TT[0], u * P:(u + 1) * P], ACT.Square,
                                       accum_out=small[:, 32 + u:33 + u])
                m.then_inc(ss_ready, 1)
                nxt(4)
                act.wait_ge(qkT_ps, h + 1)
                act.activation(qkT.rearrange("p u i -> p (u i)"), ps[:, XY[0], :], IDT).then_inc(qkT_ready, 1)
                for d in range(2):
                    act.wait_ge(de_ready, h + 1)
                    act.activation(eD[:, d * 512:(d + 1) * 512], eD[:, d * 512:(d + 1) * 512], ACT.Exp).then_inc(e_ready, 1)
                act.wait_ge(e_ready, h * 2 + 2)
                for d in range(2):
                    for v in range(2):
                        col = (4 * d + 2 * v + d) * P + (P - 1) * (1 - d)
                        m = act.activation(Kt[:, d, v, :], qkn[:, 2 + d, :], IDT, scale=eD[:, col:col + 1])
                m.then_inc(ktail_ready, 1)
                nxt(5)
                for d in range(2):
                    act.wait_ge(t0_ps, h * 2 + (d + 1))
                    act.activation(Tm[:, 4 * d:4 * d + 4, :].rearrange("p u i -> p (u i)"), ps[:, TT[d], :],
                                   IDT).then_inc(t0_ready, 1)
                for l in range(LV):
                    for d in range(2):
                        act.wait_ge(tt_ps, at_level(h, l, d))
                        act.activation(Sm[:, 4 * d:4 * d + 4, :].rearrange("p u i -> p (u i)"), ps[:, TT[d], :],
                                       IDT).then_inc(s_ready, 1)
                    if l == 2:
                        nxt(6)
                for d in range(2):
                    act.wait_ge(u0_ps, h * 2 + (d + 1))
                    act.activation(Vn[:, 4 * d:4 * d + 4, :].rearrange("p (v c) i -> p v c i", v=2)[:, :, d, :],
                                   ps[:, XY[d], 0:256].rearrange("p (v i) -> p v i", v=2), IDT).then_inc(u0_ready, 1)
                for d in range(2):
                    act.wait_ge(ks_ps, h * 4 + (2 * d + 2))
                    for v in range(2):
                        u = 4 * d + 2 * v + 1 - d
                        m = act.activation(QSs[:, 2 * v + 1 - d, :], ps[:, TT[d], 256 + v * P:256 + (v + 1) * P], IDT,
                                           scale=cols[:, 3, u:u + 1])
                    m.then_inc(qs_ready, 1)
                for d in range(2):
                    act.wait_ge(v1_ps, h * 2 + (d + 1))
                    act.activation(Vn[:, 4 * d:4 * d + 4, :].rearrange("p (v c) i -> p v c i", v=2)[:, :, 1 - d, :],
                                   ps[:, XY[d], 0:256].rearrange("p (v i) -> p v i", v=2), IDT).then_inc(v1_ready, 1)
                act.wait_ge(o_ready, h + 1)
                act.wait_ge(ss_ready, h + 1)
                for u in range(4):
                    m = act.activation(junk[:, u * P:(u + 1) * P], Osb[:, u, :], ACT.Square, accum_out=small[:, 48 + u:49 + u])
                m.then_inc(oss_ready, 1)
                if more:
                    conv_inputs(h + 1)
                act.wait_ge(oT_ps, h + 1)
                act.activation(oT[:, ds(h * 2, 2), :], ps[:, TT[0], :].rearrange("p (v t) -> p v t", v=2), IDT,
                               scale=misc[:, 32:33]).then_inc(oT_ready, 1)

            act.sem_inc(fm_done, 2)
            act.sem_inc(oss_ready, 1)
            act.sem_inc(bT_ready, 1)
            act.wait_ge(params_ready, 1)
            ch.link(act.activation(cond, misc[:, 0:KT], ACT.Tanh, scale=0.5))
            act.wait_ge(mod_ready, 1)
            pre_norm(0)
            split_hi(act, n_ab, 1, 0, m_ab, 1, 0, 0)
            act.wait_ge(ab_dve, 1)
            act.activation(abw[:, 2, :], abw[:, 1, :], ACT.Tanh, scale=0.5)
            ch.link(act.activation(abw[:, 3, :], abw[:, 0, :], ACT.Abs))
            act.activation(small[:, 2:3], small[:, 0:1], ACT.Exp)
            act.activation(abw[:, 3, :], abw[:, 3, :], ACT.Exp, scale=-1.0).then_inc(ab_act, 1)
            act.wait_ge(ab_dve, 2)
            act.activation(abw[:, 5, :], abw[:, 4, :], ACT.Ln).then_inc(ab_act, 1)
            act.wait_ge(tbl_ready, 1)
            act.activation(tbl[:, 3, :, :], tbl[:, 0, :, :], ACT.Exp).then_inc(ab_act, 1)
            for j in range(6):
                head_hi(0, j)
            head_hi(1, 0)
            act.wait_ge(rows_stored, 64)
            conv_inputs(0)
            with act.Fori(0, KH - 2) as h:
                core(h, lambda j: head_hi(h + 1, j) if j < 6 else head_hi(h + 2, 0))
            core(KH - 2, lambda j: head_hi(KH - 1, j) if j < 6 else None)
            core(KH - 1, lambda j: None, False)
            stream(n_dout, m_dout, VH, LOOPM, oT)
            post(0)
            pre_norm(1)
            gateup(n_gu0, m_gu0, 0, LOOPM, 3)
            act.wait_ge(hid_ready, 2 + FT // 2)
            stream(n_dn0, m_dn0, FT, LOOPM, hid)
            post(1)
            pre_norm(2)

            def square(n0, m0, q0, evacuate):
                def pair(i, r, after):
                    split_hi(act, n0, 4, 2 * r + 1, m0, 4, 2 * r + 1, i)
                    if after:
                        split_hi(act, n0, 4, 2 * after[1], m0, 4, 2 * after[1], after[0])
                    act.wait_ge(w_used, i * 4 + (m0 + 2 * r + 2))
                    evacuate(i, r)

                split_hi(act, n0, 4, 0, m0, 4, 0, 0)
                with act.Fori(0, 3) as i:
                    pair(i, 0, (i, 1))
                    pair(i, 1, (i + 1, 0))
                pair(3, 0, (3, 1))
                pair(3, 1, None)

            act.wait_ge(x_stored, 32)
            square(n_sin, m_sin, 0, lambda i, r: act.activation(
                uT[:, ds(i * 4 + 2 * r, 2), :], ps[:, r, :].rearrange("p (b t) -> p b t", b=2), IDT).then_inc(fm_done, 1))

            act.wait_ge(s5_dve_a, 1)
            act.activation(s5w[:, 5, :], s5w[:, 3, :], ACT.Tanh, scale=0.5).then_inc(s5_act_a, 1)
            act.wait_ge(s5_dve_a, 2)
            act.activation(s5w[:, 9, :], s5w[:, 8, :], ACT.Sin, scale=TWO_PI)
            act.activation(s5w[:, 10, :], s5w[:, 8, :], ACT.Sin, scale=TWO_PI / 2).then_inc(s5_act_a, 1)

            def bu_operands(j):
                act.wait_ge(bcT_ps, j + 2)
                act.wait_ge(bu_ps, j * 8 + 1)
                act.activation(bT.rearrange("p n i -> p (n i)"), ps[:, 0, :], IDT)
                act.activation(uj, uT[:, ds(j, 1), :].rearrange("p o t -> p (o t)"), IDT).then_inc(bT_ready, 1)

            def s5_tile(j, more):
                for q in range(8):
                    act.wait_ge(ang_ready, j * 8 + (q + 1))
                    act.wait_ge(psin_ready, j * 8 + (q + 1))
                    act.wait_ge(pcos_ready, j * 8 + (q + 1))
                    t = trig[:, q % 4]
                    act.activation(angabs[:, q % 2, :], ang[:, q % 2, :], ACT.Abs).then_inc(abs_done, 1)
                    act.activation(t[:, 1, :], ang[:, q % 2, :], ACT.Sin, scale=TWO_PI)
                    act.activation(t[:, 2, :], ang[:, q % 2, :], ACT.Sin, scale=-TWO_PI)
                    act.wait_ge(abs_done, j * 8 + (q + 1))
                    act.activation(t[:, 0, :], angabs[:, q % 2, :], ACT.Sin, scale=-TWO_PI,
                                   bias=small[:, 60:61]).then_inc(trig_ready, 1)
                if more:
                    bu_operands(j + 1)

            bu_operands(0)
            with act.Fori(0, NJ - 1) as j:
                s5_tile(j, True)
            s5_tile(NJ - 1, False)
            act.wait_ge(ysum_ready, NJ + 1)
            for half in range(2):
                act.activation(ysb[:, 8 * half:8 * half + 8, :], ysb[:, 8 * half:8 * half + 8, :], ACT.Gelu).then_inc(gelu_done, 1)
            for half in range(2):
                act.wait_ge(gelu_done, half + 1)
                act.activation(hhi[:, 8 * half:8 * half + 8, :], ysb[:, 8 * half:8 * half + 8, :], IDT).then_inc(h_hi, 1)

            def glu_out(i, r):
                act.activation(fth[:, r, :], ps[:, r, :], ACT.Tanh, scale=0.5).then_inc(glu_tanh, 1)

            square(n_glu, m_glu, 8, glu_out)
            act.wait_ge(fm_done, 2 + 16)
            stream(n_sout, m_sout, KT, 0, ysb)
            post(2)
            pre_norm(3)
            gateup(n_gu1, m_gu1, FT // 2, 0, FT // 4)
            act.wait_ge(hid_ready, 2 + FT)
            stream(n_dn1, m_dn1, FT, 0, hid)
            post(3)

        @block.vector
        def _(dve):
            ch = Chain(dve, dves)
            link = ch.link
            tt, ts, stt = dve.tensor_tensor, dve.tensor_scalar, dve.scalar_tensor_tensor

            def finish_mod(f):
                layer, chunks, _ = FINALS[f]
                dve.wait_ge(mod_ps, f + 1)
                lo, n = chunks[0] * KT, len(chunks) * KT
                m = tt(modc[:, layer, lo:lo + n], ps[:, 7, 0:n], modb[:, layer, lo:lo + n], ALU.add)
                m.then_inc(mod_ready, 1)
                dve.wait_ge(mod_ready, f + 1)

            def gate_col(s):
                layer, sub = SUB[s]["layer"], SUB[s]
                tt(gwcol[:, s, :], mod_cols(layer, sub["gt"]), norm_col(sub["post"], layer), ALU.mult).then_inc(gw_col, 1)

            def post(s, eps):
                dve.wait_ge(ss_out, s + 1)
                link(dve.tensor_reduce(small[:, 16:18], small[:, 8:16].rearrange("p (c n) -> p c n", c=2), AX_X, ALU.add))
                link(ts(small[:, 16:18], small[:, 16:18], 1.0 / D, eps, ALU.mult, ALU.add))
                newton(ch, dve, small[:, 18:20], small[:, 16:18], small[:, 20:22])
                dve.wait_ge(gw_landed, 16 * s + 16)
                dve.wait_ge(x_landed, 16 * (s + 2))
                for c in range(NT):
                    for n in range(4):
                        m = stt(out=ptmp[:, c, 512 * n:512 * (n + 1)], in0=ps[:, 4 * c + n, :],
                                scalar=small[:, 18 + c:19 + c], in1=gwrow_of[s][:, 512 * n:512 * (n + 1)],
                                op0=ALU.mult, op1=ALU.mult)
                    link(m)
                    tt(xbuf[:, c, :], xbuf[:, c, :], ptmp[:, c, :], ALU.add).then_inc(x_new, 1)

            def pre_norm(s):
                layer, sub = SUB[s]["layer"], SUB[s]
                stt(out=acol, in0=mod_cols(layer, sub["sc"]), scalar=1.0, in1=norm_col(sub["pre"], layer),
                    op0=ALU.add, op1=ALU.mult)
                dve.wait_ge(ss_x, s + 1)
                link(ts(small[:, 26:28], small[:, 24:26], 1.0 / D, EPS, ALU.mult, ALU.add))
                newton(ch, dve, small[:, 28:30], small[:, 26:28], small[:, 30:32])
                dve.sem_inc(rstd_x, 1)
                ts(xn[:, 1, :], xbuf[:, 1, :], small[:, 29:30], None, ALU.mult).then_inc(xn_ready, 1)
                for b in range(1, KT // 2, 2):
                    dve.wait_ge(xnT_ps, 8 * s + b + 1)
                    for k in (2 * b, 2 * b + 1):
                        m = ts(hfull[k // 4][:, k % 4, :], ps[:, b, (k % 2) * T:(k % 2 + 1) * T], acol[:, k:k + 1],
                               mod_cols(layer, sub["sh"])[:, k:k + 1], ALU.mult, ALU.add)
                m.then_inc(h_dve, 1)
                for q in range(4):
                    dve.wait_ge(h_hi, H_HI[s] + q + 1)
                    k4 = slice(4 * q, 4 * q + 4)
                    m = tt(hlo[:, k4, :], hfull[q], hhi[:, k4, :].bitcast(F32), ALU.subtract)
                m.then_inc(h_ready, 1)

            def stream(n0, m0, kts, lm, src, acc, mods):
                for nb, mb, kb_, trips, per, first, last in plan(n0, m0, kts, lm):
                    def body(i):
                        for j in range(4):
                            stage_lo(dve, src[:, ds(i * 4 + (kb_ + j), 1), :].rearrange("p o t -> p (o t)"),
                                     mb, 4, j, i)
                            split_lo(dve, nb, per, w_at(per == 8, j), mb, 4, j, i)
                            if per == 8:
                                mod_acc(dve, nb, i, 8, 2 * j + 1, acc[:, j % 2, :], i * 2 + (kb_ // 2 + j // 2))
                    run(dve, trips, body)

            def gateup(n0, m0, q0, lm, lp):
                parts = ([(n0, 16, m0, q0, lm)] if lm else []) + [(n0 + 16 * lm, 8, m0 + 8 * lm, q0 + 2 * lm, lp)]

                def tile(part, i, r, j):
                    nb, nper, mb, q, _ = part
                    jn = (nper // 2) * r
                    split_lo(dve, nb, nper, jn + w_at(nper == 16, j), mb, 8, 4 * r + j, i)
                    if nper == 16:
                        mod_acc(dve, nb, i, 16, jn + 2 * j + 1, macc4[:, j, :], i * 2 + r)

                def pair(part, i, r, after):
                    _, _, mb, q, _ = part
                    for j in range(1, 4):
                        tile(part, i, r, j)
                    dve.wait_ge(gate_tanh, i * 2 + (q + r + 1))
                    stt(out=ftt[:, r, :], in0=fth[:, r, :], scalar=1.0, in1=ps[:, r, :], op0=ALU.add,
                        op1=ALU.mult).then_inc(gate_used, 1)
                    if after:
                        tile(*after, 0)
                    dve.wait_ge(gate_used, i * 2 + (q + r + 3))
                    dve.wait_ge(w_used, i * 8 + (mb + 4 * r + 4))
                    tt(hid[:, ds(i * 4 + 2 * (q - q0 + r), 2), :], ftt[:, r, :].rearrange("p (b t) -> p b t", b=2),
                       ps[:, 2 + r, :].rearrange("p (b t) -> p b t", b=2), ALU.mult).then_inc(hid_ready, 1)

                tile(parts[0], 0, 0, 0)
                for n, part in enumerate(parts):
                    trips = part[4]
                    with dve.Fori(0, trips - 1) as i:
                        pair(part, i, 0, (part, i, 1))
                        pair(part, i, 1, (part, i + 1, 0))
                    pair(part, trips - 1, 0, (part, trips - 1, 1))
                    pair(part, trips - 1, 1, (parts[n + 1], 0, 0) if n + 1 < len(parts) else None)

            def head_lo(h, j):
                split_lo(dve, n_head, PER_HEAD, j, m_head, 6, j, h)

            def head_mod(h, j):
                mod_acc(dve, n_head, h, PER_HEAD, 6 + j, macc[:, j, :], h)

            def load_convw(h):
                for t, first in ((0, 0), (1, KH)):
                    dve.tensor_copy(convh[:, t, :], convw[:, :, ds(h + first, 1)].rearrange("p j o -> p (j o)"))
                link(dve.tensor_copy(convh[:, 2:4, :].rearrange("p t j -> p j t"), convw[:, :, ds(h * 2 + 2 * KH, 2)]))

            def core(h, nxt, mod):
                load_convw(h)
                dve.tensor_copy(cols, tbl[:, :, ds(h, 1), :].rearrange("p k o u -> p k (o u)"))
                for t2 in range(2):
                    dve.wait_ge(cbuf_ready, h * 2 + (t2 + 1))
                    for j in range(CK):
                        for t in (2 * t2, 2 * t2 + 1):
                            y, x = yact[:, t * T:(t + 1) * T], cbuf[:, t, j:j + T]
                            if j == 0:
                                m = ts(y, x, convh[:, t, 0:1], None, ALU.mult)
                            else:
                                ch.after(1 if j < CK - 1 or t % 2 == 0 else 0)
                                m = stt(out=y, in0=x, scalar=convh[:, t, j:j + 1], in1=y, op0=ALU.mult, op1=ALU.add)
                            if j < CK - 1:
                                ch.mark(m)
                    if t2 == 0:
                        nxt(1)
                m.then_inc(conv_done, 1)
                nxt(2)
                dve.wait_ge(silu_tanh, h + 1)
                dve.wait_ge(conv_done, h + 1)
                stt(out=yact, in0=eD, scalar=1.0, in1=yact, op0=ALU.add, op1=ALU.mult).then_inc(act_done, 1)
                dve.wait_ge(z_tanh, h + 1)
                zview = lambda v: v.rearrange("p (c v i) -> p v c i", c=2, v=2)
                for v in range(2):
                    m = stt(out=zg[:, 2 * v:2 * v + 2, :], in0=zth.rearrange("p (c v) i -> p v c i", v=2)[:, v],
                            scalar=1.0, in1=zview(ps[:, Z_BANK, :])[:, v], op0=ALU.add, op1=ALU.mult)
                m.then_inc(zg_ready, 1)
                nxt(3)
                dve.wait_ge(rows_landed, h * 64 + 64)
                dve.wait_ge(act_done, h + 1)
                for u in range(8):
                    m = ts(eD[:, u * P:(u + 1) * P], grow[:, u, :], cols[:, 0, u:u + 1], 0.0, ALU.subtract, ALU.min)
                m.then_inc(de_ready, 1)
                dve.wait_ge(ss_ready, h + 1)
                link(ts(small[:, 36:40], small[:, 32:36], 4.0 * EPS, None, ALU.add))
                newton(ch, dve, small[:, 40:44], small[:, 36:40], small[:, 44:48])
                tt(qkn, ps[:, TT[0], :].rearrange("p (u i) -> p u i", u=4), bc(small[:, 40:44], P),
                   ALU.mult).then_inc(qkn_ready, 1)
                for d in range(2):
                    m = tt(Vb[:, 4 * d:4 * d + 4, :], ps[:, TT[1], :].rearrange("p (u i) -> p u i", u=4),
                           bc(cols[:, 1, 4 * d:4 * d + 4], P), ALU.mult)
                m.then_inc(vb_ready, 1)
                nxt(4)
                dve.wait_ge(kk_ps, h + 1)
                for d in range(2):
                    for m_ in range(2):
                        m = tt(km[:, d, m_, :, :], ps[:, K_BANK, m_ * 256:(m_ + 1) * 256].rearrange("p (c i) -> p c i", c=2),
                               rep(mkq[:, d, m_, :], 2), ALU.mult)
                m.then_inc(km_ready, 1)
                dve.wait_ge(km_ready, h + 1)
                for d in range(2):
                    dve.wait_ge(eb_ready, h * 2 + (d + 1))
                    for v in range(2):
                        u = 4 * d + 2 * v
                        m = tt(Bm[:, u:u + 2, :], Bm[:, u:u + 2, :], km[:, d, 0, :, :], ALU.mult)
                    link(m)
                    link(tt(Sm[:, 4 * d:4 * d + 4, :], Bm[:, 4 * d:4 * d + 4, :], rep(m1[:, d, :], 4), ALU.mult))
                    tt(Sm[:, 4 * d:4 * d + 4, :], Sm[:, 4 * d:4 * d + 4, :], rep(ident, 4), ALU.add).then_inc(s0_ready, 1)
                for l in range(LV):
                    for d in range(2):
                        dve.wait_ge(x_ps, at_level(h, l, d))
                        tt(Xm[:, d, :, :], ps[:, XY[d], 0:256].rearrange("p (u n) -> p u n", u=4),
                           rep(mlv[:, l, d, :], 4), ALU.mult).then_inc(xm_ready, 1)
                    for d in range(2):
                        dve.wait_ge(y_ps, at_level(h, l, d))
                        t = changed(Tm[:, 4 * d:4 * d + 4, :], l, d)
                        tt(t, t, ps[:, XY[d], 256:512].rearrange("p (u n b) -> p u n b", u=4, b=2 << l),
                           ALU.add).then_inc(t_ready, 1)
                    if l == 0:
                        nxt(5)
                    if l in (1, 2):
                        mod(l - 1)
                    if l == 3:
                        nxt(6)
                for d in range(2):
                    dve.wait_ge(st_ps, h * 2 + (d + 1))
                    dve.tensor_copy(Ssb[:, d, :, :].rearrange("p v i -> p (v i)"), ps[:, TT[d], 0:256]).then_inc(st_ready, 1)
                for d in range(2):
                    dve.wait_ge(ks_ps, h * 4 + (2 * d + 1))
                    for v in range(2):
                        u = 4 * d + 2 * v + 1 - d
                        m = stt(out=R1[:, d, v, :], in0=ps[:, XY[d], 256 + v * P:256 + (v + 1) * P],
                                scalar=cols[:, 2, u:u + 1], in1=Vb[:, u, :], op0=ALU.mult, op1=ALU.add)
                    m.then_inc(r1_ready, 1)
                dve.wait_ge(o_ps, h + 2)
                dve.wait_ge(qs_ready, h * 2 + 2)
                tt(Osb, ps[:, K_BANK, :].rearrange("p (u i) -> p u i", u=4), QSs, ALU.add).then_inc(o_ready, 1)
                dve.wait_ge(oss_ready, h + 2)
                link(ts(small[:, 52:56], small[:, 48:52], 1.0 / P, EPS, ALU.mult, ALU.add))
                newton(ch, dve, small[:, 56:60], small[:, 52:56], small[:, 44:48])
                dve.wait_ge(o_ready, h + 1)
                link(tt(Osb, Osb, bc(small[:, 56:60], P), ALU.mult))
                tt(Osb, Osb, zg, ALU.mult).then_inc(og_ready, 1)

            dve.sem_inc(gate_used, 2)
            dve.sem_inc(hid_ready, 2)
            for free, n in ((pcos_ready, 4), (z_ready, 2), (ysum_ready, 1), (cj_ready, 1)):
                dve.sem_inc(free, n)
            dve.wait_ge(params_T, 1)
            dve.tensor_copy(normc, ps[:, 0, 0:P])
            dve.tensor_copy(modb[:, 0, :], ps[:, 0, P:P + 96])
            dve.tensor_copy(modb[:, 1, :], ps[:, 0, 2 * P:2 * P + 96])
            link(dve.tensor_copy(misc, ps[:, 0, 3 * P:3 * P + 33]))
            cw = convw.rearrange("p j t -> p (j t)")
            dve.tensor_copy(cw[:, 0:P], ps[:, 1, 0:P])
            dve.tensor_copy(cw[:, P:2 * P], ps[:, 1, P:2 * P])
            dve.tensor_copy(cw[:, 2 * P:320], ps[:, 1, 2 * P:2 * P + 64])
            dve.tensor_scalar(small[:, 60:61], ones[:, 0:1], math.pi / 2, None, ALU.mult)
            ts(misc[:, 32:33], misc[:, 32:33], 0.5, None, ALU.mult).then_inc(params_ready, 1)
            dve.wait_ge(acts, 1)
            link(stt(out=cond, in0=cond, scalar=1.0, in1=misc[:, 0:KT], op0=ALU.add, op1=ALU.mult))
            link(ts(cond, cond, 0.5, None, ALU.mult))
            dve.wait_ge(macc_zero, 1)
            for j in range(2):
                mod_acc(dve, 0, 0, 2, j, macc[:, j, :], 0)
            with dve.Fori(0, KT - 1) as k:
                for j in range(2):
                    mod_acc(dve, 2, k, 2, j, macc[:, j, :], k + 1)
            finish_mod(0)
            pre_norm(0)
            split_lo(dve, n_ab, 1, 0, m_ab, 1, 0, 0)

            dve.wait_ge(w_used, 1)
            ts(abw[:, 0, :], ps[:, 4, 0:T], small[:, 1:2], None, ALU.add)
            dve.tensor_copy(abw[:, 1, :], ps[:, 4, 0:T]).then_inc(ab_dve, 1)
            dve.wait_ge(ab_act, 1)
            ts(abw[:, 2, :], abw[:, 2, :], 0.5, 0.5, ALU.mult, ALU.add)
            ts(abw[:, 4, :], abw[:, 3, :], 1.0, None, ALU.add).then_inc(ab_dve, 1)
            dve.wait_ge(ab_dve, 2)
            link(dve.reciprocal(abw[:, 6, :], abw[:, 4, :]))
            link(ts(abw[:, 7, :], abw[:, 4, :], -1.0, None, ALU.add))
            link(tt(abw[:, 7, :], abw[:, 3, :], abw[:, 7, :], ALU.subtract))
            link(tt(abw[:, 7, :], abw[:, 7, :], abw[:, 6, :], ALU.mult))
            dve.wait_ge(ab_act, 2)
            link(tt(abw[:, 5, :], abw[:, 5, :], abw[:, 7, :], ALU.add))
            link(stt(out=abw[:, 0, :], in0=abw[:, 0, :], scalar=0.0, in1=abw[:, 5, :], op0=ALU.max, op1=ALU.add))
            link(ts(abw[:, 0, :], abw[:, 0, :], small[:, 2:3], -1.0, ALU.mult, ALU.mult))
            for d in range(2):
                r0 = 64 * d
                for c in range(NT):
                    lo, hi = c * P, (c + 1) * P
                    src = abw[r0:r0 + 64, 0, lo:hi]
                    dst = abw[r0:r0 + 64, 1, lo:hi]
                    if d == 1:
                        src, dst = src[:, ::-1], dst[:, ::-1]
                    m = dve.tensor_tensor_scan(dst, ones[r0:r0 + 64, 0:1].to_broadcast([64, P]), src, 0.0,
                                               ALU.mult, ALU.add)
            m.then_inc(ab_dve, 1)
            dve.wait_ge(gT_ps, 1)
            for d in range(2):
                for c in range(NT):
                    out4 = lambda kind: tbl[:, kind, :, :].rearrange("p h (d v c) -> p d c h v", d=2, v=2)[:, d, c]
                    for n, kind, r0 in ((c, 0, 64 * d + 32), (2 + c, 2, 64 * d)):
                        m = dve.tensor_copy(out4(kind), ps[:, 5, n * P + r0:n * P + r0 + 32].rearrange("p (h v) -> p h v", v=2))
            link(m)
            link(ts(tbl[:, 1, :, :], tbl[:, 2, :, :], 0.5, None, ALU.mult))
            dve.sem_inc(tbl_ready, 1)
            dve.wait_ge(ab_act, 3)
            link(stt(out=tbl[:, 2, :, :], in0=tbl[:, 2, :, :], scalar=-1.0, in1=tbl[:, 3, :, :], op0=ALU.mult, op1=ALU.mult))
            link(ts(tbl[:, 3, :, :], tbl[:, 3, :, :], DK_SCALE, None, ALU.mult))

            dve.wait_ge(macc_zero, 2)
            for j in range(6):
                head_lo(0, j)
            for j in range(2):
                head_mod(0, j)
            head_lo(1, 0)
            with dve.Fori(0, KH - 2) as h:
                ch.enter(h, HEAD_LINKS)
                core(h, lambda j: head_lo(h + 1, j) if j < 6 else head_lo(h + 2, 0), lambda j: head_mod(h + 1, j))
                ch.leave(HEAD_LINKS, KH - 2)
            core(KH - 2, lambda j: head_lo(KH - 1, j) if j < 6 else None, lambda j: head_mod(KH - 1, j))
            finish_mod(1)
            gate_col(0)
            core(KH - 1, lambda j: None, lambda j: None)
            dve.wait_ge(macc_zero, 3)
            stream(n_dout, m_dout, VH, LOOPM, oT, macc, True)
            post(0, EPS)
            finish_mod(2)
            gate_col(1)
            pre_norm(1)
            dve.wait_ge(macc_zero, 4)
            gateup(n_gu0, m_gu0, 0, LOOPM, 3)
            finish_mod(3)
            gate_col(2)
            dve.wait_ge(macc_zero, 5)
            stream(n_dn0, m_dn0, FT, LOOPM, hid, macc4, True)
            post(1, 4.0 * EPS)
            finish_mod(4)
            gate_col(3)
            pre_norm(2)

            def square(n0, m0, evacuate):
                def pair(i, r, after):
                    split_lo(dve, n0, 4, 2 * r + 1, m0, 4, 2 * r + 1, i)
                    if after:
                        split_lo(dve, n0, 4, 2 * after[1], m0, 4, 2 * after[1], after[0])
                    evacuate(i, r)

                split_lo(dve, n0, 4, 0, m0, 4, 0, 0)
                with dve.Fori(0, 3) as i:
                    pair(i, 0, (i, 1))
                    pair(i, 1, (i + 1, 0))
                pair(3, 0, (3, 1))
                pair(3, 1, None)

            square(n_sin, m_sin, lambda i, r: None)

            W = lambda n: s5w[:, n, :]
            dve.wait_ge(s5_in, 16 * 11)
            x2, k2, r2, p2, q2 = (s5w[:, 2, n:n + 2] for n in (0, 2, 4, 6, 8))
            link(ts(x2, x2, -87.3, 88.7, ALU.max, ALU.min))
            link(ts(k2, x2, 1.0 / math.log(2.0), ROUND, ALU.mult, ALU.add))
            link(ts(k2, k2, -ROUND, None, ALU.add))
            link(stt(out=r2, in0=k2, scalar=-0.693359375, in1=x2, op0=ALU.mult, op1=ALU.add))
            link(stt(out=r2, in0=k2, scalar=2.12194440e-4, in1=r2, op0=ALU.mult, op1=ALU.add))
            link(ts(p2, r2, 1.0 / 5040.0, None, ALU.mult))
            for f in (720.0, 120.0, 24.0, 6.0, 2.0, 1.0):
                link(stt(out=p2, in0=p2, scalar=1.0 / f, in1=r2, op0=ALU.add, op1=ALU.mult))
            link(ts(p2, p2, 1.0, None, ALU.add))
            link(ts(q2.bitcast(I32), k2, 127.0, 8388608.0, ALU.add, ALU.mult))
            link(tt(p2, p2, q2, ALU.mult))
            step = p2.unsqueeze(2).to_broadcast([P, 2, 64])
            e2 = lambda n: W(n).rearrange("p (e s) -> p e s", e=2)
            link(tt(e2(3), e2(0), step, ALU.mult))
            dve.sem_inc(s5_dve_a, 1)
            link(tt(e2(4), e2(1), step, ALU.mult))
            link(ts(W(6), W(4), 1.0 / (2 * math.pi), ROUND, ALU.mult, ALU.add))
            link(ts(W(6), W(6), -ROUND, None, ALU.add))
            link(stt(out=W(7), in0=W(6), scalar=-6.28125, in1=W(4), op0=ALU.mult, op1=ALU.add))
            link(stt(out=W(7), in0=W(6), scalar=-(2 * math.pi - 6.28125), in1=W(7), op0=ALU.mult, op1=ALU.add))
            link(ts(W(8), W(7), 1.0 / (2 * math.pi), 0.5, ALU.mult, ALU.min))
            link(ts(W(8), W(8), -0.5, None, ALU.max))
            dve.sem_inc(s5_dve_a, 1)
            dve.wait_ge(s5_act_a, 1)
            link(ts(W(11), W(5), -1.0, 1.0, ALU.mult, ALU.add))
            link(dve.reciprocal(W(12), W(11)))
            link(stt(out=W(13), in0=W(5), scalar=2.0, in1=W(12), op0=ALU.mult, op1=ALU.mult))
            link(stt(out=W(14), in0=W(5), scalar=1.0, in1=W(12), op0=ALU.add, op1=ALU.mult))
            dve.wait_ge(s5_act_a, 2)
            link(tt(W(15), W(10), W(10), ALU.mult))
            link(tt(W(15), W(15), W(14), ALU.mult))
            link(stt(out=W(15), in0=W(15), scalar=-2.0, in1=W(13), op0=ALU.mult, op1=ALU.add))
            link(tt(W(16), W(14), W(9), ALU.mult))
            link(tt(W(17), W(0), W(0), ALU.mult))
            link(tt(W(18), W(1), W(1), ALU.mult))
            link(tt(W(17), W(17), W(18), ALU.add))
            link(dve.reciprocal(W(18), W(17)))
            link(tt(W(19), W(15), W(0), ALU.mult))
            link(tt(W(20), W(16), W(1), ALU.mult))
            link(tt(W(19), W(19), W(20), ALU.add))
            link(tt(W(19), W(19), W(18), ALU.mult))
            link(tt(W(21), W(16), W(0), ALU.mult))
            link(tt(W(22), W(15), W(1), ALU.mult))
            link(tt(W(21), W(21), W(22), ALU.subtract))
            link(tt(W(21), W(21), W(18), ALU.mult))
            dve.sem_inc(s5_dve, 1)
            dve.wait_ge(s5_psT, 1)
            for n in range(4):
                link(dve.tensor_copy(s5p[:, n, :], ps[:, 2, n * P:(n + 1) * P]))
            link(ts(s5p[:, 1, GP:2 * GP], s5p[:, 1, GP:2 * GP], -1.0, None, ALU.mult))
            fac = [s5p[:, 2 + r, :].unsqueeze(2).to_broadcast([P, P, Q]) for r in range(2)]
            b3 = [bnat[:, r, :].rearrange("p (g c) -> p g c", c=Q) for r in range(2)]
            y3 = [ysb[:, 8 * r:8 * r + 8, :].rearrange("p k t -> p (k t)").rearrange("p (g c) -> p g c", c=Q) for r in range(2)]
            link(tt(y3[0], b3[1], fac[1], ALU.mult))
            link(tt(y3[1], b3[0], fac[1], ALU.mult))
            for r in range(2):
                link(tt(b3[r], b3[r], fac[0], ALU.mult))
            link(tt(b3[0], b3[0], y3[0], ALU.subtract))
            link(tt(b3[1], b3[1], y3[1], ALU.add))
            dve.sem_inc(s5_ready, 1)
            dve.wait_ge(s5_act, 1)
            ph, rr_, dd = colj[:, 0:8], colj[:, 8:16], colj[:, 16:17]

            def column(dst, n, j):
                link(dve.tensor_copy(dst.rearrange("p (d g) -> p d g", d=2),
                                     s5p[:, n, :].rearrange("p (d g) -> p d g", d=2)[:, :, ds(j * 4, 4)]))

            def angle(j, q, first=False):
                g, d = q // 2, q % 2
                f = ph[:, 4 * d + g:4 * d + g + 1]
                if not (first and q == 0):
                    dve.wait_ge(ang_ready, j * 8 + q)
                link(ts(kb, iota, f, ROUND, ALU.mult, ALU.add))
                link(ts(kc, kb, -ROUND, None, ALU.add))
                if not first:
                    dve.wait_ge(trig_ready, j * 8 + (q - 1))
                stt(out=ang[:, q % 2, :], in0=iota, scalar=f, in1=kc, op0=ALU.mult, op1=ALU.subtract)\
                    .then_inc(ang_ready, 1)

            def products(j, q):
                tr = trig[:, q % 4]
                bu = ps[:, 2 + q % 2, :].rearrange("p (n t) -> p n t", n=2)
                dve.wait_ge(trig_ready, j * 8 + (q + 1))
                dve.wait_ge(bu_ps, j * 8 + (q + 2))
                tt(tprod[:, q % 2, 0], rep(tr[:, 0, :], 2), bu, ALU.mult)
                tt(tprod[:, q % 2, 1], tr[:, 1:3, :], bu[:, ::-1, :], ALU.mult).then_inc(t_prod, 1)

            def c_operands(j):
                dve.wait_ge(bcT_ps, j + 2)
                for sgn in range(2):
                    m = tt(cj[:, sgn, :].rearrange("p (n i) -> p n i", n=4), ps[:, 1, :].rearrange("p (n i) -> p n i", n=4),
                           rep(gmask[:, sgn, :], 4), ALU.mult)
                m.then_inc(cj_ready, 1)

            def s5_tile(j, more):
                for q in range(8):
                    g, d = q // 2, q % 2
                    if q < 6:
                        angle(j, q + 2)
                    elif more:
                        if q == 6:
                            dve.wait_ge(ang_ready, j * 8 + 8)
                            column(ph, 1, j + 1)
                        angle(j + 1, q - 6)
                    if q < 7:
                        products(j, q + 1)
                    dve.wait_ge(zin_ready, j * 8 + (q + 1))
                    dve.wait_ge(psin_ready, j * 8 + (q + 3))
                    dve.wait_ge(pcos_ready, j * 8 + (q + 3))
                    r = rr_[:, 4 * d + g:4 * d + g + 1].to_broadcast([P, T])
                    for n in range(2):
                        o, i_ = zst[:, q % 2, n, :], zin[:, q % 2, n, :]
                        if d == 1:
                            o, i_ = o[:, ::-1], i_[:, ::-1]
                        m = dve.tensor_tensor_scan(o, r, i_, 0.0, ALU.mult, ALU.add)
                    m.then_inc(z_ready, 1)
                    dve.wait_ge(z_ready, j * 8 + (q + 3))
                    dve.wait_ge(ymm, j * 8 + (q + 1))
                    tt(pcos[:, q % 2], rep(trig[:, q % 4, 0, :], 2), zst[:, q % 2], ALU.mult).then_inc(pcos_ready, 1)
                if more:
                    column(rr_, 0, j + 1)
                dve.wait_ge(ysum_ready, j + 1)
                link(dve.tensor_copy(dd, misc[:, ds(j + KT, 1)]))
                if more:
                    products(j + 1, 0)
                dve.wait_ge(ymm, j * 8 + 10)
                stt(out=ysb[:, ds(j, 1), :].rearrange("p o t -> p (o t)"), in0=uT[:, ds(j, 1), :].rearrange("p o t -> p (o t)"),
                    scalar=dd, in1=ps[:, 4, 0:T], op0=ALU.mult, op1=ALU.add).then_inc(ysum_ready, 1)
                if more:
                    c_operands(j + 1)

            column(ph, 1, 0)
            column(rr_, 0, 0)
            angle(0, 0, True)
            angle(0, 1, True)
            products(0, 0)
            c_operands(0)
            with dve.Fori(0, NJ - 1) as j:
                ch.enter(j, S5_LINKS)
                s5_tile(j, True)
                ch.leave(S5_LINKS, NJ - 1)
            s5_tile(NJ - 1, False)
            for half in range(2):
                dve.wait_ge(h_hi, H_HI[3] - 2 + half + 1)
                s_ = slice(8 * half, 8 * half + 8)
                tt(hlo[:, s_, :], ysb[:, s_, :], hhi[:, s_, :].bitcast(F32), ALU.subtract).then_inc(glu_h, 1)

            def glu_out(i, r):
                dve.wait_ge(glu_tanh, i * 2 + (r + 1))
                y = ysb[:, ds(i * 4 + 2 * r, 2), :]
                stt(out=y.rearrange("p b t -> p (b t)"), in0=fth[:, r, :], scalar=1.0,
                    in1=y.rearrange("p b t -> p (b t)"), op0=ALU.add, op1=ALU.mult).then_inc(fm_done, 1)

            dve.wait_ge(gelu_done, 2)
            square(n_glu, m_glu, glu_out)
            stream(n_sout, m_sout, KT, 0, ysb, None, False)
            post(2, 4.0 * EPS)
            pre_norm(3)
            gateup(n_gu1, m_gu1, FT // 2, 0, FT // 4)
            stream(n_dn1, m_dn1, FT, 0, hid, None, False)
            post(3, 4.0 * EPS)


_INS = ["x", "c", "mod_w", "mod_b", "norm_pre_mix", "norm_post_mix", "norm_pre_ffn", "norm_post_ffn", "dn_w_in",
        "dn_conv_w", "dn_a_log", "dn_dt_bias", "dn_norm_w", "dn_w_out", "s5_w_in", "s5_lam_re", "s5_lam_im",
        "s5_log_step", "s5_b_re", "s5_b_im", "s5_c_re", "s5_c_im", "s5_d", "s5_w_glu", "s5_w_out", "ffn_w_gate",
        "ffn_w_up", "ffn_w_down"]


def kernel(**inputs):
    import numpy as np
    import concourse.bacc as bacc
    from concourse.bass_utils import run_bass_kernel_spmd

    nc = bacc.Bacc("TRN2", target_bir_lowering=False, num_devices=1)
    arrays, aps = {}, {}
    for name in _INS:
        arrays[f"in_{name}"] = np.ascontiguousarray(inputs[name])
        aps[name] = nc.dram_tensor(f"in_{name}", arrays[f"in_{name}"].shape, F32, kind="ExternalInput").ap()
    out = nc.dram_tensor("out", arrays["in_x"].shape, F32, kind="ExternalOutput").ap()
    trunk(nc, aps, out)
    result = run_bass_kernel_spmd(nc, [arrays], core_ids=[0])
    return result.results[0]["out"]
```
